# Optimizing a Trainium2 kernel written in Bass

```python
import jax, jax.numpy as jnp
from jax import lax
import numpy as np

D_MODEL = 1024
BATCH = 1
SEQ = 256
DEPTH = 2

HEAD_DIM = 64
N_Q_HEADS = 8
N_KV_HEADS = 2
Q_PER_KV = N_Q_HEADS // N_KV_HEADS
ATTN_WIDTH = N_Q_HEADS * HEAD_DIM
KV_WIDTH = N_KV_HEADS * HEAD_DIM
CONV_WIDTH = D_MODEL - ATTN_WIDTH
MIX_WIDTH = ATTN_WIDTH + CONV_WIDTH
N_MIX_HEADS = MIX_WIDTH // HEAD_DIM
Q_END = ATTN_WIDTH
K_END = Q_END + KV_WIDTH
V_END = K_END + KV_WIDTH
CB_END = V_END + CONV_WIDTH
CC_END = CB_END + CONV_WIDTH
IN_WIDTH = CC_END + CONV_WIDTH
WINDOW = 128
ATTN_BLOCK = 128
ROPE_THETA = 10000.0
CONV_K = 3
D_FF = 3584
N_EXPERTS = 8
TOP_K = 2
MOE_BLOCK = 128
N_DENSE = (DEPTH + 1) // 2
N_MOE = DEPTH // 2
NORM_EPS = 1e-5
NEG_INF = -1e30
MAX_POS_OFFSET = 4096

kernel_name = 'hybrid_swa_sink_shortconv_moe_trunk'

def rms_norm(x, w):
    xf = x.astype(jnp.float32)
    var = jnp.mean(xf * xf, axis=-1, keepdims=True)
    return (xf * lax.rsqrt(var + NORM_EPS) * w.astype(jnp.float32)).astype(x.dtype)

def rope_tables(positions):
    inv_freq = ROPE_THETA ** (-jnp.arange(0, HEAD_DIM, 2, dtype=jnp.float32) / HEAD_DIM)
    ang = positions.astype(jnp.float32)[..., None] * inv_freq
    return jnp.cos(ang)[:, :, None, :], jnp.sin(ang)[:, :, None, :]

def apply_rope(t, cos, sin):
    half = HEAD_DIM // 2
    tf = t.astype(jnp.float32)
    t1, t2 = tf[..., :half], tf[..., half:]
    return jnp.concatenate([t1 * cos - t2 * sin, t2 * cos + t1 * sin], axis=-1).astype(t.dtype)

def sliding_window_attention(q, k, v, sinks):
    B, S = q.shape[0], q.shape[1]
    nb = S // ATTN_BLOCK
    qb = q.reshape(B, nb, ATTN_BLOCK, N_KV_HEADS, Q_PER_KV, HEAD_DIM)

    def with_prev(t):
        tb = t.reshape(B, nb, ATTN_BLOCK, N_KV_HEADS, HEAD_DIM)
        prev = jnp.pad(tb[:, :-1], ((0, 0), (1, 0), (0, 0), (0, 0), (0, 0)))
        return jnp.concatenate([prev, tb], axis=2)

    kk, vv = with_prev(k), with_prev(v)
    s = jnp.einsum('bnqkgd,bnskd->bkgnqs', qb, kk).astype(jnp.float32) * (HEAD_DIM ** -0.5)
    blk = jnp.arange(nb)[:, None, None] * ATTN_BLOCK
    q_pos = blk + jnp.arange(ATTN_BLOCK)[None, :, None]
    k_pos = blk - ATTN_BLOCK + jnp.arange(2 * ATTN_BLOCK)[None, None, :]
    dist = q_pos - k_pos
    mask = (dist >= 0) & (dist < WINDOW) & (k_pos >= 0)
    s = jnp.where(mask, s, NEG_INF)
    sink = sinks.astype(jnp.float32).reshape(N_KV_HEADS, Q_PER_KV)[None, :, :, None, None, None]
    m = jnp.maximum(jnp.max(s, axis=-1, keepdims=True), sink)
    p = jnp.exp(s - m)
    p = p / (jnp.sum(p, axis=-1, keepdims=True) + jnp.exp(sink - m))
    o = jnp.einsum('bkgnqs,bnskd->bnqkgd', p.astype(v.dtype), vv)
    return o.reshape(B, S, ATTN_WIDTH)

def causal_depthwise_conv(u, w):
    S = u.shape[1]
    up = jnp.pad(u, ((0, 0), (CONV_K - 1, 0), (0, 0)))
    y = w[0] * up[:, 0:S]
    for i in range(1, CONV_K):
        y = y + w[i] * up[:, i:i + S]
    return y

def hybrid_mixer(h, cos, sin, w_in, sinks, conv_w, head_norm_w, w_out):
    B, S, _ = h.shape
    proj = h @ w_in
    q = apply_rope(proj[..., :Q_END].reshape(B, S, N_Q_HEADS, HEAD_DIM), cos, sin)
    k = apply_rope(proj[..., Q_END:K_END].reshape(B, S, N_KV_HEADS, HEAD_DIM), cos, sin)
    v = proj[..., K_END:V_END].reshape(B, S, N_KV_HEADS, HEAD_DIM)
    attn = sliding_window_attention(q, k, v, sinks)
    gate_b = proj[..., V_END:CB_END]
    gate_c = proj[..., CB_END:CC_END]
    hc = proj[..., CC_END:]
    conv = gate_b * causal_depthwise_conv(gate_c * hc, conv_w)
    y = jnp.concatenate([attn, conv], axis=-1).reshape(B, S, N_MIX_HEADS, HEAD_DIM)
    y = rms_norm(y, head_norm_w.reshape(N_MIX_HEADS, HEAD_DIM)).reshape(B, S, MIX_WIDTH)
    return y @ w_out

def swiglu(h, w_gate, w_up, w_down):
    return (jax.nn.silu(h @ w_gate) * (h @ w_up)) @ w_down

def moe_swiglu(h, router_w, w_gate, w_up, w_down):
    B, S, D = h.shape
    N = B * S
    t = h.reshape(N, D)
    logits = (t @ router_w).astype(jnp.float32)
    top_logits, top_idx = lax.top_k(logits, TOP_K)
    gates = jax.nn.softmax(top_logits, axis=-1)
    flat_e = top_idx.reshape(-1)
    flat_tok = jnp.repeat(jnp.arange(N, dtype=jnp.int32), TOP_K)
    flat_g = gates.reshape(-1)
    order = jnp.argsort(flat_e)
    sorted_e = flat_e[order]
    sizes = jnp.bincount(flat_e, length=N_EXPERTS)
    padded = (sizes + MOE_BLOCK - 1) // MOE_BLOCK * MOE_BLOCK
    group_start = jnp.cumsum(sizes) - sizes
    padded_end = jnp.cumsum(padded)
    padded_start = padded_end - padded
    n_assign = N * TOP_K
    rank = jnp.arange(n_assign, dtype=jnp.int32) - group_start[sorted_e]
    dest = padded_start[sorted_e] + rank
    n_rows = -(-n_assign // MOE_BLOCK) * MOE_BLOCK + N_EXPERTS * MOE_BLOCK
    n_blocks = n_rows // MOE_BLOCK
    row_tok = jnp.full((n_rows,), N, dtype=jnp.int32).at[dest].set(flat_tok[order])
    row_gate = jnp.zeros((n_rows,), jnp.float32).at[dest].set(flat_g[order])
    blk_e = jnp.minimum(jnp.searchsorted(padded_end, jnp.arange(n_blocks) * MOE_BLOCK, side='right'),
                        N_EXPERTS - 1)
    t_pad = jnp.concatenate([t, jnp.zeros((1, D), t.dtype)], axis=0)
    xs = t_pad[row_tok].reshape(n_blocks, MOE_BLOCK, D)

    def expert_block(args):
        xb, e = args
        return swiglu(xb, w_gate[e], w_up[e], w_down[e])

    ys = lax.map(expert_block, (xs, blk_e)).reshape(n_rows, D)
    ys = ys * row_gate[:, None].astype(ys.dtype)
    out = jnp.zeros((N + 1, D), ys.dtype).at[row_tok].add(ys)[:N]
    return out.reshape(B, S, D)

def setup_inputs(seed: int = 0) -> dict:
    key = jax.random.key(seed)
    ks = jax.random.split(key, 18)
    f32 = jnp.float32
    nrm = lambda k, shape, scale: jax.random.normal(k, shape, f32) * scale
    x = jax.random.normal(ks[0], (BATCH, SEQ, D_MODEL), f32)
    offset = jax.random.randint(ks[1], (BATCH,), 0, MAX_POS_OFFSET, dtype=jnp.int32)
    positions = offset[:, None] + jnp.arange(SEQ, dtype=jnp.int32)[None, :]
    return {
        'x': x,
        'positions': positions,
        'attn_norm_w': 1.0 + nrm(ks[2], (DEPTH, D_MODEL), 0.02),
        'w_in': nrm(ks[3], (DEPTH, D_MODEL, IN_WIDTH), D_MODEL ** -0.5),
        'attn_sinks': nrm(ks[4], (DEPTH, N_Q_HEADS), 0.5),
        'conv_w': nrm(ks[5], (DEPTH, CONV_K, CONV_WIDTH), CONV_K ** -0.5),
        'head_norm_w': 1.0 + nrm(ks[6], (DEPTH, MIX_WIDTH), 0.02),
        'w_out': nrm(ks[7], (DEPTH, MIX_WIDTH, D_MODEL), MIX_WIDTH ** -0.5),
        'ffn_norm_w': 1.0 + nrm(ks[8], (DEPTH, D_MODEL), 0.02),
        'dense_w_gate': nrm(ks[9], (N_DENSE, D_MODEL, D_FF), D_MODEL ** -0.5),
        'dense_w_up': nrm(ks[10], (N_DENSE, D_MODEL, D_FF), D_MODEL ** -0.5),
        'dense_w_down': nrm(ks[11], (N_DENSE, D_FF, D_MODEL), D_FF ** -0.5),
        'router_w': nrm(ks[12], (N_MOE, D_MODEL, N_EXPERTS), D_MODEL ** -0.5),
        'moe_w_gate': nrm(ks[13], (N_MOE, N_EXPERTS, D_MODEL, D_FF), D_MODEL ** -0.5),
        'moe_w_up': nrm(ks[14], (N_MOE, N_EXPERTS, D_MODEL, D_FF), D_MODEL ** -0.5),
        'moe_w_down': nrm(ks[15], (N_MOE, N_EXPERTS, D_FF, D_MODEL), D_FF ** -0.5),
        'final_norm_w': 1.0 + nrm(ks[16], (D_MODEL,), 0.02),
    }

def reference(x, positions, attn_norm_w, w_in, attn_sinks, conv_w, head_norm_w, w_out, ffn_norm_w,
              dense_w_gate, dense_w_up, dense_w_down, router_w, moe_w_gate, moe_w_up, moe_w_down,
              final_norm_w):
    cos, sin = rope_tables(positions)
    for l in range(DEPTH):
        h = rms_norm(x, attn_norm_w[l])
        x = x + hybrid_mixer(h, cos, sin, w_in[l], attn_sinks[l], conv_w[l], head_norm_w[l], w_out[l])
        h = rms_norm(x, ffn_norm_w[l])
        if l % 2 == 0:
            i = l // 2
            x = x + swiglu(h, dense_w_gate[i], dense_w_up[i], dense_w_down[i])
        else:
            i = l // 2
            x = x + moe_swiglu(h, router_w[i], moe_w_gate[i], moe_w_up[i], moe_w_down[i])
    return rms_norm(x, final_norm_w)


_drawn_inputs = setup_inputs


def setup_inputs(seed=0):
    import zlib

    import numpy as np

    out = dict(_drawn_inputs(seed))
    spreads = {}
    factors = {'attn_sinks': 22.439, 'final_norm_w': 8.157}
    for name, (base, spread) in spreads.items():
        noise = np.random.default_rng([zlib.crc32(name.encode()), seed]).standard_normal(out[name].shape)
        drawn = base * np.exp(spread * noise) if base else spread * noise
        out[name] = __import__('jax').numpy.asarray(drawn.astype(out[name].dtype))
    for name, factor in factors.items():
        out[name] = (out[name] * factor).astype(out[name].dtype)
    return out
```

```python
from contextlib import ExitStack

import numpy as np
import concourse.bass as bass
from concourse import mybir

F32 = mybir.dt.float32
F32R = mybir.dt.float32r
BF16 = mybir.dt.bfloat16
I32 = mybir.dt.int32
U32 = mybir.dt.uint32
ALU = mybir.AluOpType
ACT = mybir.ActivationFunctionType
AX = mybir.AxisListType.X

P = 128
HEAD = 64
N_Q, N_KV = 8, 2
CONV_K = 3
THETA = 10000.0
EPS = 1e-5
NEG = -1e30
TWO_PI = 2 * np.pi

RAW = 6
SPLIT = 3
UNIT = 2048
SCATTER = (6, 7, 3, 1)


def parts_of_two_pi(bits, n):
    rest, found = TWO_PI, []
    for _ in range(n - 1):
        step = 2.0 ** (np.floor(np.log2(rest)) - bits + 1)
        found.append(float(np.floor(rest / step) * step))
        rest -= found[-1]
    return found + [float(np.float32(rest))]


def trunk(nc, x, positions, attn_norm_w, w_in, attn_sinks, conv_w, head_norm_w, w_out, ffn_norm_w,
          dense_w_gate, dense_w_up, dense_w_down, router_w, moe_w_gate, moe_w_up, moe_w_down,
          final_norm_w, out):
    _, S, D = x.shape
    L = w_in.shape[0]
    IN = w_in.shape[2]
    F = dense_w_gate.shape[2]
    E = moe_w_gate.shape[1]
    T = S // P
    K = D // P
    AW = N_Q * HEAD
    CW = D - AW
    K0, V0 = AW, AW + N_KV * HEAD
    B0, C0, H0 = V0 + N_KV * HEAD, V0 + N_KV * HEAD + CW, V0 + N_KV * HEAD + 2 * CW
    NH = D // HEAD
    CH = 512
    STEPS = F // CH
    HALF = HEAD // 2
    assert T == 2 and K == 8 and F % CH == 0 and L == 2 and IN == 4 * CH + CH // 2

    IN_UNITS = 9
    MIX_UNITS = IN_UNITS + 4
    FFN_UNITS = 6 * STEPS
    SMALL = 3 * L + T + 2
    MIX = [0, MIX_UNITS + FFN_UNITS]
    FFN = [MIX_UNITS, 2 * MIX_UNITS + FFN_UNITS]

    with ExitStack() as ctx:
        def sb(name, shape, dt=F32, at=ctx):
            return at.enter_context(nc.sbuf_tensor(name, shape, dt))

        def sem(name):
            return ctx.enter_context(nc.semaphore(name))

        ps = ctx.enter_context(nc.psum_tensor("ps", [P, 8, CH], F32))

        raw = [sb(f"raw{i}", [P, UNIT]) for i in range(RAW)]
        hi = [sb(f"hi{i}", [P, UNIT], F32R) for i in range(SPLIT)]
        lo = [sb(f"lo{i}", [P, UNIT], F32R) for i in range(SPLIT)]
        x_sb = sb("x_sb", [P, T, D])
        xn = sb("xn", [P, T, D])
        xT_hi = sb("xT_hi", [P, K, S], F32R)
        xT_lo = sb("xT_lo", [P, K, S], F32R)
        ident = sb("ident", [P, P])
        mask = sb("mask", [P, 2 * P])
        norm_rows = sb("norm_rows", [6 * K, P])
        norm_cols = sb("norm_cols", [P, 6 * K])
        w_row = sb("w_row", [P, D])
        sinks = sb("sinks", [P, L, N_Q])
        pos = sb("pos", [P, T], I32)
        freq = sb("freq", [P, HALF])
        ang = sb("ang", [P, T, HALF])
        turns = sb("turns", [P, T, HALF])
        turns_hi = sb("turns_hi", [P, T, HALF])
        cos = sb("cos", [P, T, HALF])
        sin = sb("sin", [P, T, HALF])
        ssq = sb("ssq", [P, T])
        var = sb("var", [P, T])
        rstd = sb("rstd", [P, T])
        half_neg = sb("half_neg", [P, T * NH])
        ssq_h = sb("ssq_h", [P, T, NH])
        var_h = sb("var_h", [P, T, NH])
        rstd_h = sb("rstd_h", [P, T, NH])
        smax = sb("smax", [P, T, N_Q])
        m_sb = sb("m_sb", [P, T, N_Q])
        neg_m = sb("neg_m", [P, T, N_Q])
        sink_d = sb("sink_d", [P, T, N_Q])
        sink_e = sb("sink_e", [P, T, N_Q])
        row_sum = sb("row_sum", [P, T, N_Q])
        den = sb("den", [P, T, N_Q])
        rden = sb("rden", [P, T, N_Q])
        router = sb("router", [P, K, E])
        router_hi = sb("router_hi", [P, K, E], F32R)
        router_lo = sb("router_lo", [P, K, E], F32R)
        before = sb("before", [P, P], BF16)
        ones = sb("ones", [P, P], BF16)
        slot_no = sb("slot_no", [P, P])
        expert_no = sb("expert_no", [P, E])
        logits = sb("logits", [P, T, E])
        top = sb("top", [P, T, 8])
        top_at = sb("top_at", [P, T, 8], U32)
        top_f = sb("top_f", [P, T, 2])
        gap = sb("gap", [P, T])
        e2 = sb("e2", [P, T])
        one_e2 = sb("one_e2", [P, T])
        gates = sb("gates", [P, T, 2])
        first = sb("first", [P, T, E])
        second = sb("second", [P, T, E])
        chosen = sb("chosen", [P, T, E])
        chosen_b = sb("chosen_b", [P, T, E], BF16)
        gate = sb("gate", [P, T, 2 * E])
        rank = sb("rank", [P, T, 2 * E + 1])
        rank1 = sb("rank1", [P, T, E])
        count = sb("count", [P, 1])
        passes_i = sb("passes_i", [P, 1], I32)

        mixer_region = ExitStack()
        proj = sb("proj", [P, T, IN], at=mixer_region)
        k_twice = sb("k_twice", [P, T, N_KV, 2, HEAD], at=mixer_region)
        qT = sb("qT", [P, N_Q // 2, S], at=mixer_region)
        kT = sb("kT", [P, N_KV, S], at=mixer_region)
        sc = [sb("sc0", [P, 2, 4, P], at=mixer_region), sb("sc1", [P, 2, 4, 2 * P], at=mixer_region)]
        pT = sb("pT", [P, 3 * N_Q, P], at=mixer_region)
        u_shift = [sb(f"u_shift{i}", [P, T, CW], at=mixer_region) for i in (1, 2)]
        conv_row = sb("conv_row", [P, CONV_K, CW], at=mixer_region)
        mixer_region.close()
        silu = sb("silu", [P, 1024])
        hid = sb("hid", [P, 1024])
        hT_hi = sb("hT_hi", [P, 4, S], F32R)
        hT_lo = sb("hT_lo", [P, 4, S], F32R)
        t_hi = sb("t_hi", [P, T, D], F32R)
        t_lo = sb("t_lo", [P, T, D], F32R)
        y_hi = sb("y_hi", [P, D], F32R)
        y_lo = sb("y_lo", [P, D], F32R)
        pick = sb("pick", [P, T, P], F32R)
        pickT = sb("pickT", [P, T, P], F32R)

        s_raw = [sem(f"raw_landed{i}") for i in range(RAW)]
        s_hi, s_lo, s_used = sem("hi_written"), sem("lo_written"), sem("unit_used")
        s_x, s_small, s_wrow, s_conv = sem("x_landed"), sem("small_landed"), sem("w_row_landed"), sem("conv_w_landed")
        s_const = sem("constants_built")
        s_cols, s_colsb = sem("norm_cols_turned"), sem("norm_cols_copied")
        s_ang, s_trig = sem("angles_ready"), sem("sin_cos_ready")
        s_ssq, s_rstd, s_xn = sem("squares_summed"), sem("rstd_ready"), sem("rows_normed")
        s_hsq, s_ssqh, s_rstdh = sem("head_squares_ready"), sem("head_squares_summed"), sem("head_rstd_ready")
        s_turn, s_thi, s_tlo = sem("rows_turned"), sem("xT_hi_written"), sem("xT_lo_written")
        s_pjo, s_rope = sem("proj_copied"), sem("rope_done")
        s_qkT, s_qkA, s_qkD = sem("qk_turned"), sem("qk_copied_by_act"), sem("qk_copied_by_dve")
        s_score, s_masked, s_negm, s_exp, s_esink = (sem("scores_ready"), sem("scores_masked"), sem("max_ready"),
                                                     sem("exp_done"), sem("sink_exp_done"))
        s_pT, s_pTA, s_pTD = sem("probs_turned"), sem("probsT_copied_by_act"), sem("probsT_copied_by_dve")
        s_o, s_attn = sem("attention_ready"), sem("attention_normed")
        s_conv_done, s_shift = sem("conv_done"), sem("shift_landed")
        s_silu, s_hid = sem("silu_done"), sem("hidden_ready")
        s_hT, s_hhi, s_hlo = sem("hidden_turned"), sem("hT_hi_written"), sem("hT_lo_written")
        s_y0, s_yhi, s_ylo = sem("y_first_half"), sem("y_hi_written"), sem("y_lo_written")
        s_rw, s_logit, s_top, s_e2, s_chosen, s_prefix, s_route = (
            sem("router_split"), sem("logits_ready"), sem("top_found"), sem("gap_exp_done"), sem("chosen_ready"),
            sem("prefix_ready"), sem("routes_ready"))
        s_tok, s_tokhi, s_toklo = sem("tokens_scaled"), sem("tokens_hi"), sem("tokens_lo")
        s_pick, s_gath, s_xhi, s_xlo = sem("pick_built"), sem("tokens_gathered"), sem("xe_hi_written"), sem("xe_lo_written")
        s_pkT, s_pickT, s_scat, s_added = (sem("pick_turned"), sem("pickT_copied"), sem("y_scattered"),
                                           sem("residual_added"))
        s_out = sem("out_stored")
        s_dvec, s_poolc = sem("dve_chain"), sem("pool_chain")

        def no(u):
            return u[0] + RAW * u[1]

        def load_unit(sp, u, view):
            s, d = u
            if s >= RAW:
                sp.wait_ge(s_lo, no(u) - RAW + 1)
            k = view.shape[1]
            dst = raw[s % RAW][:].rearrange("p (k n) -> p k n", k=k)
            sp.dma_start(dst, view).then_inc(s_raw[s % RAW], 16)

        def split_hi(act, u):
            s, d = u
            act.wait_ge(s_raw[s % RAW], 16 * (s // RAW + 1 + d))
            if s >= SPLIT:
                act.wait_ge(s_used, no(u) - SPLIT + 1)
            act.copy(hi[s % SPLIT][:], raw[s % RAW][:]).then_inc(s_hi, 1)

        def split_lo(dve, u):
            s, d = u
            dve.wait_ge(s_hi, no(u) + 1)
            dve.tensor_tensor(lo[s % SPLIT][:], raw[s % RAW][:], hi[s % SPLIT][:].bitcast(F32),
                              ALU.subtract).then_inc(s_lo, 1)

        def halves(u, k):
            s = u[0]
            return [h[s % SPLIT][:].rearrange("p (k n) -> p k n", k=k) for h in (hi, lo)]

        def gate_unit(base, c, h, d=0):
            return (base + h, d) if c == 0 else (base + 4 + h, d)

        def up_unit(base, c, h, d=0):
            return (base + 2 + h, d) if c == 0 else (base + 6 + h, d)

        def down_unit(base, h, d=0):
            return (base + 8 + h, d)

        def last_unit(base, h, d=0):
            return (base + FFN_UNITS - 2 + h, d)

        block = ctx.enter_context(nc.Block())

        @block.sync
        def _(sp):
            sp.dma_start(x_sb[:], x.rearrange("a (t p) d -> p (a t) d", p=P)).then_inc(s_x, 16)

            def mixer(l):
                src = w_in[l].rearrange("(k p) n -> p k n", p=P)
                for c in range(4):
                    for h in range(2):
                        load_unit(sp, (MIX[l] + 2 * c + h, 0), src[:, 4 * h:4 * h + 4, c * CH:(c + 1) * CH])
                load_unit(sp, (MIX[l] + 8, 0), src[:, :, 4 * CH:IN])
                src = w_out[l].rearrange("(k p) n -> p k n", p=P)
                for c in range(2):
                    for h in range(2):
                        load_unit(sp, (MIX[l] + IN_UNITS + 2 * c + h, 0),
                                  src[:, 4 * h:4 * h + 4, c * CH:(c + 1) * CH])

            def swiglu(base, gate_w, up_w, down_w, e, d0):
                def gate_up(c, col, d):
                    for h in range(2):
                        load_unit(sp, gate_unit(base, c, h, d), gate_w[:, bass.ds(K * e + 4 * h, 4), bass.ds(col, CH)])
                    for h in range(2):
                        load_unit(sp, up_unit(base, c, h, d), up_w[:, bass.ds(K * e + 4 * h, 4), bass.ds(col, CH)])

                gate_up(0, 0, d0)
                with sp.Fori(1, STEPS) as c:
                    d = d0 + (c - 1)
                    gate_up(1, CH * c, d)
                    for h in range(2):
                        load_unit(sp, down_unit(base, h, d), down_w[:, bass.ds(e * (F // P) + 4 * c - 4 + 2 * h, 2), :])
                for h in range(2):
                    load_unit(sp, last_unit(base, h, d0),
                              down_w[:, bass.ds(e * (F // P) + F // P - 4 + 2 * h, 2), :])

            mixer(0)
            swiglu(FFN[0], dense_w_gate.rearrange("l (k p) n -> p (l k) n", p=P),
                   dense_w_up.rearrange("l (k p) n -> p (l k) n", p=P),
                   dense_w_down.rearrange("l (k p) n -> p (l k) n", p=P), 0, 0)
            mixer(1)
            moe = (moe_w_gate.rearrange("l e (k p) n -> p (l e k) n", p=P),
                   moe_w_up.rearrange("l e (k p) n -> p (l e k) n", p=P),
                   moe_w_down.rearrange("l e (k p) n -> p (l e k) n", p=P))
            with sp.Fori(0, E) as e:
                swiglu(FFN[1], *moe, e, STEPS * e)
            sp.wait_ge(s_route, 1)
            passes = sp.value_load(passes_i[0:1, 0:1], min_val=1, max_val=2)
            with sp.If(passes > 1):
                with sp.Fori(0, E) as e:
                    swiglu(FFN[1], *moe, e, STEPS * e + STEPS * E)
            for h in range(2):
                load_unit(sp, (FFN[1] + h, passes * (STEPS * E)), moe[0][:, 4 * h:4 * h + 4, 0:CH])
            sp.wait_ge(s_xn, 7 * T)
            sp.dma_start(out.rearrange("a (t p) d -> p (a t) d", p=P), xn[:]).then_inc(s_out, 16)
            sp.wait_ge(s_out, 16)

        @block.gpsimd
        def _(pool):
            chain = [0]

            def link(ins):
                chain[0] += 1
                ins.then_inc(s_poolc, 1)
                pool.wait_ge(s_poolc, chain[0])

            pool.dma_start(w_row[:], ffn_norm_w[L - 1:L, :].partition_broadcast(P)).then_inc(s_wrow, 16)
            link(pool.memset(ident[:], 0.0))
            pool.affine_select(ident[:], ident[:], [[-1, P]], ALU.not_equal, 1.0, base=0,
                               channel_multiplier=1).then_inc(s_const, 1)
            inv_freq = np.power(np.float32(THETA), -np.arange(0, HEAD, 2, dtype=np.float32) / np.float32(HEAD))
            for i in range(HALF):
                last = pool.memset(freq[:, i:i + 1], float(inv_freq[i]))
            last.then_inc(s_const, 1)
            pool.memset(half_neg[:], -0.5)
            link(pool.memset(mask[:], 0.0))
            link(pool.affine_select(mask[:], mask[:], [[-1, 2 * P]], ALU.is_ge, NEG, base=P, channel_multiplier=1))
            link(pool.affine_select(mask[:], mask[:], [[1, 2 * P]], ALU.is_gt, NEG, base=0, channel_multiplier=-1))
            link(pool.memset(ones[:], 1.0))
            pool.affine_select(before[:], ones[:], [[1, P]], ALU.is_gt, 0.0, base=0, channel_multiplier=-1)
            pool.iota(slot_no[:], [[1, P]], base=0, channel_multiplier=0, allow_small_or_imprecise_dtypes=True)
            pool.iota(expert_no[:], [[1, E]], base=0, channel_multiplier=0,
                      allow_small_or_imprecise_dtypes=True).then_inc(s_const, 1)

            def rsqrt(i):
                pool.wait_ge(s_ssq, T * (i + 1))
                link(pool.tensor_scalar(var[:], ssq[:], 1.0 / D, EPS, ALU.mult, ALU.add))
                pool.tensor_tensor(rstd[:], var[:], half_neg[:, 0:T], ALU.pow).then_inc(s_rstd, 1)

            for l in range(L):
                rsqrt(2 * l)
                pool.dma_start(conv_row[:], conv_w[l].unsqueeze(0).partition_broadcast(P)).then_inc(s_conv, 16)
                pool.wait_ge(s_pjo, 5 * l + 5)
                u = proj[:, :, C0:H0]
                gate_b = proj[:, :, B0:C0]
                link(pool.tensor_tensor(u, u, proj[:, :, H0:IN], ALU.mult))
                for i, us in enumerate(u_shift):
                    s = i + 1
                    link(pool.memset(us[0:s, 0, :], 0.0))
                    pool.dma_start(us[s:P, :, :], proj[0:P - s, :, C0:H0]).then_inc(s_shift, 16)
                    pool.dma_start(us[0:s, 1, :], proj[P - s:P, 0, C0:H0]).then_inc(s_shift, 16)
                u1, u2 = u_shift[0][:], u_shift[1][:]
                pool.wait_ge(s_shift, 64 * (l + 1))
                pool.wait_ge(s_conv, 16 * (l + 1))

                def tap(i):
                    return conv_row[:, i, :].unsqueeze(1).to_broadcast([P, T, CW])

                link(pool.tensor_tensor(u2, u2, tap(0), ALU.mult))
                link(pool.tensor_tensor(u1, u1, tap(1), ALU.mult))
                link(pool.tensor_tensor(u2, u2, u1, ALU.add))
                link(pool.tensor_tensor(u, u, tap(2), ALU.mult))
                link(pool.tensor_tensor(u2, u2, u, ALU.add))
                pool.tensor_tensor(xn[:, :, AW:D], gate_b, u2, ALU.mult).then_inc(s_conv_done, 1)
                pool.wait_ge(s_ssqh, l + 1)
                link(pool.tensor_scalar(var_h[:], ssq_h[:], 1.0 / HEAD, EPS, ALU.mult, ALU.add))
                pool.tensor_tensor(rstd_h[:], var_h[:], half_neg[:].rearrange("p (t h) -> p t h", t=T),
                                   ALU.pow).then_inc(s_rstdh, 1)
                rsqrt(2 * l + 1)
            pool.wait_ge(s_tok, T)
            pool.dma_start(w_row[:], final_norm_w.unsqueeze(0).partition_broadcast(P)).then_inc(s_wrow, 16)
            rsqrt(4)
            pool.wait_ge(s_wrow, 32)

        @block.scalar
        def _(act):
            issued = [0]

            def ahead(n):
                for u in range(issued[0], n):
                    split_hi(act, (u, 0))
                issued[0] = max(issued[0], n)

            for l in range(L):
                for i, w in enumerate((attn_norm_w, head_norm_w, ffn_norm_w)):
                    r = K * (3 * l + i)
                    act.dma_start(norm_rows[r:r + K, :], w[l].rearrange("(k p) -> k p", p=P)).then_inc(s_small, 16)
            for t in range(T):
                act.dma_start(pos[:, t:t + 1], positions[0:1, t * P:(t + 1) * P].rearrange("a p -> p a")
                              ).then_inc(s_small, 16)
            act.dma_start(sinks[:].rearrange("p l h -> p (l h)"),
                          attn_sinks.rearrange("(a l) h -> a (l h)", a=1).partition_broadcast(P)).then_inc(s_small, 16)
            act.dma_start(router[:], router_w[0].rearrange("(k p) e -> p k e", p=P)).then_inc(s_small, 16)

            def squares(i):
                if i == 0:
                    act.wait_ge(s_x, 16)
                else:
                    act.wait_ge(s_added, 4 * i)
                for t in range(T):
                    act.activation(xn[:, t, :], x_sb[:, t, :], ACT.Square,
                                   accum_out=ssq[:, t:t + 1]).then_inc(s_ssq, 1)

            def turn_hi(j):
                for b in range(4):
                    act.wait_ge(s_turn, 4 * j + b + 1)
                    for i in range(2):
                        k = 2 * b + i
                        last = act.mul(xT_hi[:, k, :], ps[:, 4 + b, i * S:(i + 1) * S],
                                       norm_cols[:, K * j + k:K * j + k + 1])
                    last.then_inc(s_thi, 1)

            squares(0)
            ahead(2)
            act.wait_ge(s_ang, 1)
            act.activation(sin[:], ang[:], ACT.Sin)
            act.activation(cos[:], turns[:], ACT.Sin).then_inc(s_trig, 1)
            act.wait_ge(s_small, 16 * SMALL)
            act.copy(router_hi[:], router[:]).then_inc(s_rw, 1)
            act.wait_ge(s_cols, 1)
            act.copy(norm_cols[:], ps[:, 0, 0:6 * K]).then_inc(s_colsb, 1)
            act.wait_ge(s_colsb, 1)

            def mixer(l):
                base = MIX[l]
                if l:
                    squares(2 * l)
                ahead(base + 3)
                turn_hi(3 * l)
                for c in range(5):
                    done = base + min(2 * c + 1, 8)
                    ahead(done + 3)
                    act.wait_ge(s_used, done + 1)
                    for t in range(T):
                        w = min(CH, IN - c * CH)
                        last = act.copy(proj[:, t, c * CH:c * CH + w], ps[:, 2 * (c % 2) + t, 0:w])
                    last.then_inc(s_pjo, 1)
                act.wait_ge(s_qkT, l + 1)
                act.mul(qT[:, 0:2, :], ps[:, 4, :], HEAD ** -0.5).then_inc(s_qkA, 1)
                act.copy(kT[:], ps[:, 6, :]).then_inc(s_qkA, 1)
                ahead(base + IN_UNITS + 3)
                for t in range(T):
                    act.wait_ge(s_negm, T * l + t + 1)
                    for h in range(N_Q):
                        s = sc[t][:, h % 2, h // 2, :]
                        last = act.activation(s, s, ACT.Exp, bias=neg_m[:, t, h:h + 1],
                                              accum_out=row_sum[:, t, h:h + 1])
                    last.then_inc(s_exp, 1)
                    act.activation(sink_e[:, t, :], sink_d[:, t, :], ACT.Exp).then_inc(s_esink, 1)
                for i in range(3):
                    b = (6, 0, 2)[i]
                    act.wait_ge(s_pT, 6 * l + 2 * i + 1)
                    act.copy(pT[:, 8 * i:8 * i + 4, :], ps[:, b, :]).then_inc(s_pTA, 1)
                act.wait_ge(s_attn, T * (l + 1))
                act.wait_ge(s_conv_done, l + 1)
                act.activation(sc[1][:].rearrange("p a b c -> p (a b c)"),
                               xn[:].rearrange("p t d -> p (t d)"), ACT.Square).then_inc(s_hsq, 1)
                turn_hi(3 * l + 1)
                ahead(base + MIX_UNITS + 2)
                squares(2 * l + 1)
                ahead(base + MIX_UNITS + (3 if l == 0 else 2))
                turn_hi(3 * l + 2)

            def silu_step(g, u, dense):
                act.wait_ge(s_used, no(u) + 1)
                act.wait_ge(s_hid, g) if not (isinstance(g, int) and g == 0) else None
                if dense:
                    act.activation(silu[:], ps[:, 0:2, :], ACT.Silu).then_inc(s_silu, 1)
                else:
                    act.activation(silu[:, 0:CH], ps[:, 0, :], ACT.Silu).then_inc(s_silu, 1)

            def hidden_hi(base, g, gm, prev_down, dense):
                if dense:
                    act.wait_ge(s_hid, g + 1)
                    if prev_down is not None:
                        act.wait_ge(s_used, no(prev_down) + 1)
                    act.copy(hT_hi[:], hid[:]).then_inc(s_hhi, 1)
                else:
                    act.wait_ge(s_hT, gm + 1)
                    act.copy(hT_hi[:, :, 0:P], ps[:, 1, :]).then_inc(s_hhi, 1)

            def swiglu(base, g0, gm0, d0, dense, pick_e=None):
                ustart = issued[0] - base if dense else 2
                for i in range(ustart, 4):
                    split_hi(act, (base + i, d0))
                silu_step(g0, gate_unit(base, 0, 1, d0), dense)
                if pick_e is not None:
                    act.wait_ge(s_pkT, pick_e + 1)
                    act.copy(pickT[:], ps[:, 7, 0:S]).then_inc(s_pickT, 1)
                split_hi(act, (base + 4, d0))
                split_hi(act, (base + 5, d0))
                with act.Fori(1, STEPS) as c:
                    d = d0 + (c - 1)
                    b = base + 4
                    split_hi(act, (b + 2, d))
                    split_hi(act, (b + 3, d))
                    silu_step(g0 + c, gate_unit(base, 1, 1, d), dense)
                    hidden_hi(base, g0 + c - 1, gm0 + c - 1, (b - 1, d), dense)
                    for i in range(4, 8):
                        split_hi(act, (b + i, d))

            mixer(0)
            swiglu(FFN[0], 0, 0, 0, True)
            hidden_hi(FFN[0], STEPS - 1, 0, (FFN[0] + FFN_UNITS - 3, 0), True)
            issued[0] = FFN[0] + FFN_UNITS
            ahead(FFN[0] + FFN_UNITS + 2)
            mixer(1)

            for t in range(T):
                act.wait_ge(s_tok, t + 1)
                act.copy(t_hi[:, t, :], xn[:, t, :]).then_inc(s_tokhi, 1)
            act.wait_ge(s_top, 1)
            act.activation(e2[:], gap[:], ACT.Exp).then_inc(s_e2, 1)

            def gathered_hi(e):
                for i, b in enumerate((7, 6)):
                    act.wait_ge(s_gath, 2 * e + i + 1)
                    act.copy(xT_hi[:, 4 * i:4 * i + 4, 0:P], ps[:, b, :]).then_inc(s_xhi, 1)

            gathered_hi(0)
            act.wait_ge(s_route, 1)
            passes = act.value_load(passes_i[0:1, 0:1], min_val=1, max_val=2)
            with act.Fori(0, passes * E) as e:
                swiglu(FFN[1], STEPS + STEPS * e, STEPS * e, STEPS * e, False, e)
                hidden_hi(FFN[1], 0, STEPS * e + STEPS - 1, None, False)
                gathered_hi(e + 1)
                for i in range(2):
                    split_hi(act, (FFN[1] + FFN_UNITS + i, STEPS * e))
                for h in range(2):
                    if h == 0:
                        act.wait_ge(s_y0, e + 1)
                    else:
                        act.wait_ge(s_used, no(last_unit(FFN[1], 1, STEPS * e)) + 1)
                    act.copy(y_hi[:, h * CH:(h + 1) * CH], ps[:, 4 + h, :]).then_inc(s_yhi, 1)
            act.wait_ge(s_added, 12 + passes * (4 * E))
            for t in range(T):
                act.activation(xn[:, t, :], x_sb[:, t, :], ACT.Square,
                               accum_out=ssq[:, t:t + 1]).then_inc(s_ssq, 1)

        @block.vector
        def _(dve):
            issued = [0]
            chain = [0]

            def ahead(n):
                for u in range(issued[0], n):
                    split_lo(dve, (u, 0))
                issued[0] = max(issued[0], n)

            def link(ins):
                chain[0] += 1
                ins.then_inc(s_dvec, 1)
                dve.wait_ge(s_dvec, chain[0])

            def wide(ap, n):
                return ap.unsqueeze(1).to_broadcast([P, n, ap.shape[1]])

            dve.wait_ge(s_small, 16 * SMALL)
            dve.wait_ge(s_const, 2)
            link(dve.tensor_copy(gap[:], pos[:]))
            for t in range(T):
                last = dve.tensor_scalar(ang[:, t, :], freq[:], gap[:, t:t + 1], None, ALU.mult)
            link(last)
            magic = 1.5 * 2 ** 23
            link(dve.tensor_scalar(turns[:], ang[:], 1 / TWO_PI, magic, ALU.mult, ALU.add))
            link(dve.tensor_scalar(turns[:], turns[:], magic, None, ALU.subtract))
            link(dve.tensor_scalar(turns_hi[:], turns[:], magic * 4096, None, ALU.add))
            link(dve.tensor_scalar(turns_hi[:], turns_hi[:], magic * 4096, None, ALU.subtract))
            link(dve.tensor_tensor(turns[:], turns[:], turns_hi[:], ALU.subtract))
            for part in parts_of_two_pi(12, 3):
                for n in (turns_hi, turns):
                    link(dve.scalar_tensor_tensor(ang[:], n[:], -part, ang[:], ALU.mult, ALU.add))
            pi = float(np.nextafter(np.float32(np.pi), np.float32(0)))
            link(dve.tensor_scalar(ang[:], ang[:], pi, -pi, ALU.min, ALU.max))
            link(dve.scalar_tensor_tensor(turns[:], ang[:], -1.0, ang[:], ALU.mult, ALU.max))
            dve.tensor_scalar(turns[:], turns[:], -1.0, float(np.pi / 2), ALU.mult, ALU.add).then_inc(s_ang, 1)
            dve.wait_ge(s_rw, 1)
            dve.tensor_tensor(router_lo[:], router[:], router_hi[:].bitcast(F32), ALU.subtract).then_inc(s_rw, 1)

            def normed(i):
                dve.wait_ge(s_rstd, i + 1)
                for t in range(T):
                    dve.tensor_scalar(xn[:, t, :], x_sb[:, t, :], rstd[:, t:t + 1], None,
                                      ALU.mult).then_inc(s_xn, 1)

            def turn_lo(j):
                for b in range(4):
                    dve.wait_ge(s_thi, 4 * j + b + 1)
                    for i in range(2):
                        k = 2 * b + i
                        last = dve.scalar_tensor_tensor(xT_lo[:, k, :], ps[:, 4 + b, i * S:(i + 1) * S],
                                                        norm_cols[:, K * j + k:K * j + k + 1],
                                                        xT_hi[:, k, :].bitcast(F32), ALU.mult, ALU.subtract)
                    last.then_inc(s_tlo, 1)

            def rope(l, t):
                qk = proj[:, t, 0:V0]
                flat = sc[1][:].rearrange("p a b c -> p (a b c)")
                by_cos, by_sin = flat[:, 0:V0], flat[:, V0:2 * V0]
                n = V0 // HALF
                dve.tensor_tensor(by_cos.rearrange("p (n d) -> p n d", d=HALF),
                                  qk.rearrange("p (n d) -> p n d", d=HALF), wide(cos[:, t, :], n), ALU.mult)
                link(dve.tensor_tensor(by_sin.rearrange("p (n d) -> p n d", d=HALF),
                                       qk.rearrange("p (n d) -> p n d", d=HALF), wide(sin[:, t, :], n), ALU.mult))
                c, s, q = (a.rearrange("p (h x d) -> p h x d", x=2, d=HALF) for a in (by_cos, by_sin, qk))
                for x, op in ((0, ALU.subtract), (1, ALU.add)):
                    dve.tensor_tensor(q[:, 0:N_Q, x, :], c[:, 0:N_Q, x, :], s[:, 0:N_Q, 1 - x, :], op)
                    for i in range(2):
                        last = dve.tensor_tensor(k_twice[:, t, :, i, x * HALF:(x + 1) * HALF],
                                                 c[:, N_Q:, x, :], s[:, N_Q:, 1 - x, :], op)
                last.then_inc(s_rope, 1)

            def mixer(l):
                base = MIX[l]
                ahead(base + 2)
                normed(2 * l)
                ahead(base + 3)
                if l == 0:
                    dve.wait_ge(s_colsb, 1)
                turn_lo(3 * l)
                ahead(base + 6)
                dve.wait_ge(s_pjo, 5 * l + 2)
                dve.wait_ge(s_trig, 1)
                for t in range(T):
                    if t:
                        dve.wait_ge(s_rope, T * l + t)
                    rope(l, t)
                ahead(base + IN_UNITS + 2)
                dve.wait_ge(s_qkT, l + 1)
                dve.tensor_scalar(qT[:, 2:4, :], ps[:, 5, :], HEAD ** -0.5, None, ALU.mult).then_inc(s_qkD, 1)
                ahead(base + IN_UNITS + 3)
                for t in range(T):
                    keys = mask[:, P:2 * P] if t == 0 else mask[:]
                    if t == 0:
                        dve.wait_ge(s_score, 3 * l + 1)
                        dve.tensor_tensor(sc[0][:, 0], ps[:, 0, :], wide(keys, 4), ALU.add)
                        link(dve.tensor_tensor(sc[0][:, 1], ps[:, 1, :], wide(keys, 4), ALU.add))
                    else:
                        for i in range(2):
                            dve.wait_ge(s_score, 3 * l + 2 + i)
                            dve.tensor_tensor(sc[1][:, 0, 2 * i:2 * i + 2], ps[:, 2 + i, :], wide(keys, 2), ALU.add)
                            last = dve.tensor_tensor(sc[1][:, 1, 2 * i:2 * i + 2], ps[:, 4 + i, :], wide(keys, 2),
                                                     ALU.add)
                        link(last)
                    link(dve.tensor_reduce(smax[:, t, :].rearrange("p (i x) -> p x i", x=2), sc[t][:], AX, ALU.max))
                    link(dve.tensor_tensor(m_sb[:, t, :], smax[:, t, :], sinks[:, l, :], ALU.max))
                    link(dve.tensor_scalar(neg_m[:, t, :], m_sb[:, t, :], -1.0, None, ALU.mult))
                    dve.tensor_tensor(sink_d[:, t, :], sinks[:, l, :], neg_m[:, t, :], ALU.add).then_inc(s_negm, 1)
                for i in range(3):
                    b = (7, 1, 3)[i]
                    dve.wait_ge(s_pT, 6 * l + 2 * i + 2)
                    dve.tensor_copy(pT[:, 8 * i + 4:8 * i + 8, :], ps[:, b, :]).then_inc(s_pTD, 1)
                for t in range(T):
                    dve.wait_ge(s_exp, T * l + t + 1)
                    dve.wait_ge(s_esink, T * l + t + 1)
                    link(dve.tensor_tensor(den[:, t, :], row_sum[:, t, :], sink_e[:, t, :], ALU.add))
                    link(dve.reciprocal(rden[:, t, :], den[:, t, :]))
                    dve.wait_ge(s_o, T * l + t + 1)
                    dve.tensor_tensor(xn[:, t, 0:AW].rearrange("p (h d) -> p h d", d=HEAD),
                                      ps[:, 4 + t, :].rearrange("p (h d) -> p h d", d=HEAD),
                                      rden[:, t, :].unsqueeze(2).to_broadcast([P, N_Q, HEAD]),
                                      ALU.mult).then_inc(s_attn, 1)
                dve.wait_ge(s_hsq, l + 1)
                dve.tensor_reduce(ssq_h[:], sc[1][:].rearrange("p a b c -> p (a b c)")
                                  .rearrange("p (t h d) -> p t h d", t=T, d=HEAD), AX, ALU.add).then_inc(s_ssqh, 1)
                dve.wait_ge(s_rstdh, l + 1)
                for t in range(T):
                    y = xn[:, t, :].rearrange("p (h d) -> p h d", d=HEAD)
                    dve.tensor_tensor(y, y, rstd_h[:, t, :].unsqueeze(2).to_broadcast([P, NH, HEAD]),
                                      ALU.mult).then_inc(s_xn, 1)
                turn_lo(3 * l + 1)
                for n in range(2):
                    ahead(base + IN_UNITS + 2 * n + 4)
                    dve.wait_ge(s_used, base + IN_UNITS + 2 * n + 2)
                    for t in range(T):
                        xs = x_sb[:, t, n * CH:(n + 1) * CH]
                        dve.tensor_tensor(xs, ps[:, 2 * n + t, :], xs, ALU.add).then_inc(s_added, 1)
                normed(2 * l + 1)
                ahead(base + MIX_UNITS + (3 if l == 0 else 2))
                turn_lo(3 * l + 2)

            def hidden(g, u, dense):
                dve.wait_ge(s_used, no(u) + 1)
                dve.wait_ge(s_silu, g + 1)
                if not (isinstance(g, int) and g == 0):
                    dve.wait_ge(s_hlo, g)
                if dense:
                    dve.tensor_tensor(hid[:], ps[:, 2:4, :], silu[:], ALU.mult).then_inc(s_hid, 1)
                else:
                    dve.tensor_tensor(hid[:, 0:CH], ps[:, 2, :], silu[:, 0:CH], ALU.mult).then_inc(s_hid, 1)

            def hidden_lo(g, dense):
                dve.wait_ge(s_hhi, g + 1)
                if dense:
                    dve.tensor_tensor(hT_lo[:], hid[:], hT_hi[:].bitcast(F32), ALU.subtract).then_inc(s_hlo, 1)
                else:
                    dve.tensor_tensor(hT_lo[:, :, 0:P], ps[:, 1, :], hT_hi[:, :, 0:P].bitcast(F32),
                                      ALU.subtract).then_inc(s_hlo, 1)

            def swiglu(base, g0, d0, dense, between=None):
                ustart = issued[0] - base if dense else 2
                for i in range(ustart, 4):
                    split_lo(dve, (base + i, d0))
                split_lo(dve, (base + 4, d0))
                if between:
                    between()
                split_lo(dve, (base + 5, d0))
                hidden(g0, up_unit(base, 0, 1, d0), dense)
                with dve.Fori(1, STEPS) as c:
                    d = d0 + (c - 1)
                    b = base + 4
                    split_lo(dve, (b + 2, d))
                    split_lo(dve, (b + 3, d))
                    hidden_lo(g0 + c - 1, dense)
                    split_lo(dve, (b + 4, d))
                    split_lo(dve, (b + 5, d))
                    hidden(g0 + c, up_unit(base, 1, 1, d), dense)
                    split_lo(dve, (b + 6, d))
                    split_lo(dve, (b + 7, d))

            mixer(0)
            swiglu(FFN[0], 0, 0, True)
            hidden_lo(STEPS - 1, True)
            issued[0] = FFN[0] + FFN_UNITS
            ahead(FFN[0] + FFN_UNITS + 2)
            dve.wait_ge(s_used, FFN[0] + FFN_UNITS)
            for t in range(T):
                for h in range(2):
                    xs = x_sb[:, t, h * CH:(h + 1) * CH]
                    dve.tensor_tensor(xs, ps[:, 4 + 2 * t + h, :], xs, ALU.add).then_inc(s_added, 1)
            mixer(1)

            dve.wait_ge(s_logit, 1)
            link(dve.tensor_copy(logits[:], ps[:, 0, 0:T * E]))
            for t in range(T):
                last = dve.max(top[:, t, :], logits[:, t, :])
            link(last)
            for t in range(T):
                last = dve.max_index(top_at[:, t, :], top[:, t, :], logits[:, t, :])
            dve.tensor_tensor(gap[:], top[:, :, 1], top[:, :, 0], ALU.subtract).then_inc(s_top, 1)
            link(last)
            link(dve.tensor_copy(top_f[:], top_at[:, :, 0:2]))
            for t in range(T):
                dve.tensor_scalar(first[:, t, :], expert_no[:], top_f[:, t, 0:1], None, ALU.is_equal)
                last = dve.tensor_scalar(second[:, t, :], expert_no[:], top_f[:, t, 1:2], None, ALU.is_equal)
            link(last)
            link(dve.tensor_tensor(chosen[:], first[:], second[:], ALU.add))
            dve.tensor_copy(chosen_b[:], chosen[:]).then_inc(s_chosen, 1)
            dve.wait_ge(s_turn, 24)
            dve.wait_ge(s_wrow, 16)
            for t in range(T):
                dve.tensor_tensor(xn[:, t, :], xn[:, t, :], w_row[:], ALU.mult).then_inc(s_tok, 1)
            dve.wait_ge(s_e2, 1)
            link(dve.tensor_scalar(one_e2[:], e2[:], 1.0, None, ALU.add))
            link(dve.reciprocal(gates[:, :, 0], one_e2[:]))
            link(dve.tensor_tensor(gates[:, :, 1], gates[:, :, 0], e2[:], ALU.mult))
            for t in range(T):
                last = dve.tensor_scalar(gate[:, t, 0:E], first[:, t, :], gates[:, t, 0:1], None, ALU.mult)
            link(last)
            for t in range(T):
                last = dve.scalar_tensor_tensor(gate[:, t, 0:E], second[:, t, :], gates[:, t, 1:2],
                                                gate[:, t, 0:E], ALU.mult, ALU.add)
            link(last)
            link(dve.tensor_copy(gate[:, :, E:2 * E], gate[:, :, 0:E]))
            dve.wait_ge(s_prefix, 1)
            dve.memset(rank[:], -1.0)
            link(dve.tensor_scalar(rank1[:], ps[:, 1, 0:T * E].rearrange("p (t e) -> p t e", t=T), 1.0, None, ALU.add))
            link(dve.tensor_tensor(rank1[:], rank1[:], chosen[:], ALU.mult))
            dve.tensor_scalar(rank[:, :, 0:E], rank1[:], -1.0, None, ALU.add)
            dve.tensor_scalar(rank[:, :, E:2 * E], rank1[:], -1.0 - P, None, ALU.add)
            link(dve.tensor_reduce(count[:], ps[:, 1, T * E:(T + 1) * E], AX, ALU.max))
            link(dve.tensor_scalar(passes_i[:], count[:], float(P), 1.0, ALU.is_gt, ALU.add))
            dve.memset(count[:], 0.0).then_inc(s_route, 1)

            def build_pick(e):
                for t in range(T):
                    last = dve.tensor_scalar(pick[:, t, :], slot_no[:], rank[:, t, bass.ds(e, 1)], None, ALU.is_equal)
                last.then_inc(s_pick, 1)

            def gathered_lo(e):
                for i, b in enumerate((7, 6)):
                    dve.wait_ge(s_xhi, 2 * e + i + 1)
                    dve.tensor_tensor(xT_lo[:, 4 * i:4 * i + 4, 0:P], ps[:, b, :],
                                      xT_hi[:, 4 * i:4 * i + 4, 0:P].bitcast(F32), ALU.subtract).then_inc(s_xlo, 1)

            build_pick(0)
            for t in range(T):
                dve.wait_ge(s_tokhi, t + 1)
                dve.tensor_tensor(t_lo[:, t, :], xn[:, t, :], t_hi[:, t, :].bitcast(F32),
                                  ALU.subtract).then_inc(s_toklo, 1)
            gathered_lo(0)
            passes = dve.value_load(passes_i[0:1, 0:1], min_val=1, max_val=2)
            with dve.Fori(0, passes * E) as e:
                def next_pick():
                    dve.wait_ge(s_pkT, e + 1)
                    build_pick(e + 1)

                swiglu(FFN[1], STEPS + STEPS * e, STEPS * e, False, next_pick)
                hidden_lo(STEPS + STEPS * e + STEPS - 1, False)
                gathered_lo(e + 1)
                for i in range(2):
                    split_lo(dve, (FFN[1] + FFN_UNITS + i, STEPS * e))
                for h in range(2):
                    dve.wait_ge(s_yhi, 2 * e + h + 1)
                    dve.tensor_tensor(y_lo[:, h * CH:(h + 1) * CH], ps[:, 4 + h, :],
                                      y_hi[:, h * CH:(h + 1) * CH].bitcast(F32), ALU.subtract).then_inc(s_ylo, 1)
                dve.wait_ge(s_added, 4 * e + 12)
                for h in range(2):
                    for t in range(T):
                        i = T * h + t
                        dve.wait_ge(s_scat, 4 * e + i + 1)
                        xs = x_sb[:, t, h * CH:(h + 1) * CH]
                        dve.scalar_tensor_tensor(xs, ps[:, SCATTER[i], :], gate[:, t, bass.ds(e, 1)], xs,
                                                 ALU.mult, ALU.add).then_inc(s_added, 1)
            dve.wait_ge(s_rstd, 5)
            dve.wait_ge(s_wrow, 32)
            for t in range(T):
                dve.scalar_tensor_tensor(xn[:, t, :], x_sb[:, t, :], rstd[:, t:t + 1], w_row[:],
                                         ALU.mult, ALU.mult).then_inc(s_xn, 1)

        @block.tensor
        def _(pe):
            def three(out_ap, a_hi, a_lo, b_hi, b_lo, start, stop, **kw):
                pe.matmul(out_ap, a_hi, b_hi, start=start, stop=False, **kw)
                pe.matmul(out_ap, a_hi, b_lo, start=False, stop=False, **kw)
                return pe.matmul(out_ap, a_lo, b_hi, start=False, stop=stop, **kw)

            def ready(u):
                pe.wait_ge(s_lo, no(u) + 1)

            def turn(j):
                for t in range(T):
                    pe.wait_ge(s_xn, T * j + t + 1)
                    if t == 0 and j:
                        pe.wait_ge(s_tlo, 4 * j)
                    for k in range(K):
                        mm = pe.transpose(ps[:, 4 + k // 2, (k % 2) * S + t * P:(k % 2) * S + (t + 1) * P],
                                          xn[:, t, k * P:(k + 1) * P], ident[:])
                        if t == T - 1 and k % 2:
                            mm.then_inc(s_turn, 1)

            def rows_product(u, k0, nk, banks, first, last):
                ready(u)
                uh, ul = halves(u, nk)
                for t in range(T):
                    for k in range(nk):
                        a = slice(t * P, (t + 1) * P)
                        mm = three(ps[:, banks[t], 0:uh.shape[2]], xT_hi[:, k0 + k, a], xT_lo[:, k0 + k, a],
                                   uh[:, k], ul[:, k], first and k == 0, last and k == nk - 1)
                mm.then_inc(s_used, 1)

            def mixer(l):
                base = MIX[l]
                turn(3 * l)
                pe.wait_ge(s_tlo, 4 * (3 * l + 1))
                for c in range(5):
                    if c >= 2:
                        pe.wait_ge(s_pjo, 5 * l + c - 1)
                    banks = [2 * (c % 2) + t for t in range(T)]
                    if c < 4:
                        rows_product((base + 2 * c, 0), 0, 4, banks, True, False)
                        rows_product((base + 2 * c + 1, 0), 4, 4, banks, False, True)
                    else:
                        rows_product((base + 8, 0), 0, 8, banks, True, True)
                for t in range(T):
                    pe.wait_ge(s_rope, T * l + t + 1)
                    for i in range(4):
                        pe.transpose(ps[:, 4 + i // 2, (i % 2) * S + t * P:(i % 2) * S + (t + 1) * P],
                                     proj[:, t, i * P:(i + 1) * P], ident[:])
                    for i in range(N_KV):
                        mm = pe.transpose(ps[:, 6, i * S + t * P:i * S + (t + 1) * P],
                                          k_twice[:, t, i].rearrange("p a d -> p (a d)"), ident[:])
                mm.then_inc(s_qkT, 1)
                pe.wait_ge(s_qkA, 2 * (l + 1))
                pe.wait_ge(s_qkD, l + 1)
                pe.wait_ge(s_pjo, 5 * l + 5)
                for t in range(T):
                    for i in range(4):
                        for x in range(2):
                            rows = slice(x * HEAD, (x + 1) * HEAD)
                            if t == 0:
                                o = ps[:, x, i * P:(i + 1) * P]
                            else:
                                o = ps[:, 2 + 2 * x + i // 2, (i % 2) * S:(i % 2 + 1) * S]
                            mm = pe.matmul(o, qT[rows, i, t * P:(t + 1) * P], kT[rows, i // 2, 0:(t + 1) * P],
                                           start=True, stop=True)
                        if (t == 0 and i == 3) or (t == 1 and i % 2):
                            mm.then_inc(s_score, 1)
                for t in range(T):
                    pe.wait_ge(s_exp, T * l + t + 1)
                    for n in range(N_Q * (t + 1)):
                        h, kt = n // (t + 1), n % (t + 1)
                        b = (6, 7)[n // 4] if t == 0 else n // 4
                        mm = pe.transpose(ps[:, b, (n % 4) * P:(n % 4 + 1) * P],
                                          sc[t][:, h % 2, h // 2, kt * P:(kt + 1) * P], ident[:])
                        if n % 4 == 3:
                            mm.then_inc(s_pT, 1)
                for t in range(T):
                    pe.wait_ge(s_pTA, 3 * l + (1 if t == 0 else 3))
                    pe.wait_ge(s_pTD, 3 * l + (1 if t == 0 else 3))
                    for h in range(N_Q):
                        for kt in range(t + 1):
                            v = proj[:, kt, V0 + h // 4 * HEAD:V0 + (h // 4 + 1) * HEAD]
                            mm = pe.matmul(ps[:, 4 + t, h * HEAD:(h + 1) * HEAD],
                                           pT[:, N_Q * t + h * (t + 1) + kt, :], v, start=kt == 0, stop=kt == t)
                    mm.then_inc(s_o, 1)
                turn(3 * l + 1)
                pe.wait_ge(s_tlo, 4 * (3 * l + 2))
                for n in range(2):
                    rows_product((base + IN_UNITS + 2 * n, 0), 0, 4, [2 * n, 2 * n + 1], True, False)
                    rows_product((base + IN_UNITS + 2 * n + 1, 0), 4, 4, [2 * n, 2 * n + 1], False, True)
                turn(3 * l + 2)

            def dense_half(u, h, b0):
                ready(u)
                uh, ul = halves(u, 4)
                for j in range(4):
                    for k in range(4):
                        xk = 4 * h + k
                        w = slice(j * P, (j + 1) * P)
                        o = ps[:, b0 + j // 2, (j % 2) * S:(j % 2 + 1) * S]
                        mm = three(o, uh[:, k, w], ul[:, k, w], xT_hi[:, xk, :], xT_lo[:, xk, :],
                                   h == 0 and k == 0 and j % 2 == 0, h == 1 and k == 3, skip_group_check=True)
                mm.then_inc(s_used, 1)

            def dense_down(u, h, start, stop):
                ready(u)
                uh, ul = halves(u, 2)
                for t in range(T):
                    for n in range(2):
                        for i in range(2):
                            a = hT_hi[:, 2 * h + i, t * P:(t + 1) * P], hT_lo[:, 2 * h + i, t * P:(t + 1) * P]
                            w = slice(n * CH, (n + 1) * CH)
                            mm = three(ps[:, 4 + 2 * t + n, :], *a, uh[:, i, w], ul[:, i, w],
                                       start and h == 0 and i == 0, stop and h == 1 and i == 1)
                mm.then_inc(s_used, 1)

            def expert_half(u, h, b):
                ready(u)
                uh, ul = halves(u, 4)
                for k in range(4):
                    xk = 4 * h + k
                    mm = three(ps[:, b, :], xT_hi[:, xk, 0:P], xT_lo[:, xk, 0:P], uh[:, k], ul[:, k],
                               h == 0 and k == 0, h == 1 and k == 3)
                mm.then_inc(s_used, 1)

            def expert_down(u, h, start, stop):
                ready(u)
                uh, ul = halves(u, 2)
                for n in range(2):
                    for i in range(2):
                        w = slice(n * CH, (n + 1) * CH)
                        mm = three(ps[:, 4 + n, :], hT_hi[:, 2 * h + i, 0:P], hT_lo[:, 2 * h + i, 0:P],
                                   uh[:, i, w], ul[:, i, w], start and h == 0 and i == 0, stop and h == 1 and i == 1)
                    if stop and h == 1 and n == 0:
                        mm.then_inc(s_y0, 1)
                mm.then_inc(s_used, 1)

            def turn_hidden(g):
                pe.wait_ge(s_hid, g + 1)
                for j in range(4):
                    mm = pe.transpose(ps[:, 1, j * P:(j + 1) * P], hid[:, j * P:(j + 1) * P], ident[:])
                mm.then_inc(s_hT, 1)

            def step(base, c, g, d, dense, start_down=None, pick_e=None):
                half = dense_half if dense else expert_half
                if not (isinstance(g, int) and g == 0):
                    pe.wait_ge(s_silu, g)
                half(gate_unit(base, c, 0, d), 0, 0)
                half(gate_unit(base, c, 1, d), 1, 0)
                if pick_e is not None:
                    pe.wait_ge(s_added, 4 * pick_e + 12)
                    for t in range(T):
                        mm = pe.transpose(ps[:, 7, t * P:(t + 1) * P], pick[:, t, :].bitcast(F32), ident[:])
                    mm.then_inc(s_pkT, 1)
                if c and not dense:
                    turn_hidden(g - 1)
                if not (isinstance(g, int) and g == 0):
                    pe.wait_ge(s_hid, g)
                half(up_unit(base, c, 0, d), 0, 2)
                half(up_unit(base, c, 1, d), 1, 2)
                if c:
                    down = dense_down if dense else expert_down
                    pe.wait_ge(s_hlo, g)
                    for h in range(2):
                        down(down_unit(base, h, d), h, start_down, False)

            def swiglu(base, g0, d0, dense, pick_e=None):
                step(base, 0, g0, d0, dense, pick_e=pick_e)
                step(base, 1, g0 + 1, d0, dense, True)
                with pe.Fori(2, STEPS) as c:
                    step(base, 2, g0 + c, d0 + (c - 1), dense, False)

            pe.wait_ge(s_const, 1)
            pe.wait_ge(s_small, 16 * SMALL)
            pe.transpose(ps[:, 0, 0:6 * K], norm_rows[:], ident[0:6 * K, 0:6 * K]).then_inc(s_cols, 1)
            pe.wait_ge(s_colsb, 1)
            mixer(0)
            pe.wait_ge(s_tlo, 12)
            swiglu(FFN[0], 0, 0, True)
            pe.wait_ge(s_hlo, STEPS)
            dense_down(last_unit(FFN[0], 0), 0, False, True)
            dense_down(last_unit(FFN[0], 1), 1, False, True)
            mixer(1)

            pe.wait_ge(s_tlo, 24)
            pe.wait_ge(s_rw, 2)
            for t in range(T):
                for k in range(K):
                    a = slice(t * P, (t + 1) * P)
                    mm = three(ps[:, 0, t * E:(t + 1) * E], xT_hi[:, k, a], xT_lo[:, k, a], router_hi[:, k, :],
                               router_lo[:, k, :], k == 0, k == K - 1)
            mm.then_inc(s_logit, 1)
            pe.wait_ge(s_chosen, 1)
            pe.wait_ge(s_const, 3)
            pe.matmul(ps[:, 1, 0:E], before[:], chosen_b[:, 0, :], start=True, stop=True)
            pe.matmul(ps[:, 1, E:2 * E], ones[:], chosen_b[:, 0, :], start=True, stop=False)
            pe.matmul(ps[:, 1, E:2 * E], before[:], chosen_b[:, 1, :], start=False, stop=True)
            pe.matmul(ps[:, 1, 2 * E:3 * E], ones[:], chosen_b[:, 0, :], start=True, stop=False)
            pe.matmul(ps[:, 1, 2 * E:3 * E], ones[:], chosen_b[:, 1, :], start=False, stop=True).then_inc(s_prefix, 1)

            def gather(e):
                pe.wait_ge(s_pick, e + 1)
                for i, b in enumerate((7, 6)):
                    for k in range(4):
                        cols = slice((4 * i + k) * P, (4 * i + k + 1) * P)
                        for t in range(T):
                            pe.matmul(ps[:, b, k * P:(k + 1) * P], t_hi[:, t, cols], pick[:, t, :],
                                      start=t == 0, stop=False)
                            mm = pe.matmul(ps[:, b, k * P:(k + 1) * P], t_lo[:, t, cols], pick[:, t, :],
                                           start=False, stop=t == T - 1)
                    mm.then_inc(s_gath, 1)

            pe.wait_ge(s_toklo, T)
            gather(0)
            pe.wait_ge(s_route, 1)
            passes = pe.value_load(passes_i[0:1, 0:1], min_val=1, max_val=2)
            with pe.Fori(0, passes * E) as e:
                pe.wait_ge(s_xlo, 2 * e + 2)
                swiglu(FFN[1], STEPS + STEPS * e, STEPS * e, False, e)
                turn_hidden(STEPS + STEPS * e + STEPS - 1)
                pe.wait_ge(s_pickT, e + 1)
                gather(e + 1)
                pe.wait_ge(s_hlo, STEPS + STEPS * e + STEPS)
                expert_down(last_unit(FFN[1], 0, STEPS * e), 0, False, True)
                expert_down(last_unit(FFN[1], 1, STEPS * e), 1, False, True)
                for h in range(2):
                    pe.wait_ge(s_ylo, 2 * e + h + 1)
                    for t in range(T):
                        i = T * h + t
                        if i == 0:
                            pe.wait_ge(s_xlo, 2 * e + 4)
                        cols = slice(h * CH, (h + 1) * CH)
                        pe.matmul(ps[:, SCATTER[i], :], pickT[:, t, :], y_hi[:, cols], start=True, stop=False)
                        pe.matmul(ps[:, SCATTER[i], :], pickT[:, t, :], y_lo[:, cols], start=False,
                                  stop=True).then_inc(s_scat, 1)


_INS = ["x", "positions", "attn_norm_w", "w_in", "attn_sinks", "conv_w", "head_norm_w", "w_out", "ffn_norm_w",
        "dense_w_gate", "dense_w_up", "dense_w_down", "router_w", "moe_w_gate", "moe_w_up", "moe_w_down",
        "final_norm_w"]


def kernel(**inputs):
    import concourse.bacc as _bacc
    from concourse.bass_utils import run_bass_kernel_spmd as _run

    nc = _bacc.Bacc("TRN2", target_bir_lowering=False, num_devices=1)
    arrays, args = {}, []
    for name in _INS:
        a = np.ascontiguousarray(inputs[name])
        arrays[f"in_{name}"] = a
        args.append(nc.dram_tensor(f"in_{name}", a.shape, mybir.dt.from_np(a.dtype), kind="ExternalInput").ap())
    out = nc.dram_tensor("out_0", inputs["x"].shape, F32, kind="ExternalOutput").ap()
    trunk(nc, *args, out)
    r = _run(nc, [arrays], core_ids=[0])
    return r.results[0]["out_0"]
```

```python
from contextlib import ExitStack

import numpy as np
import concourse.bass as bass
from concourse import mybir

F32 = mybir.dt.float32
F32R = mybir.dt.float32r
BF16 = mybir.dt.bfloat16
I32 = mybir.dt.int32
U32 = mybir.dt.uint32
ALU = mybir.AluOpType
ACT = mybir.ActivationFunctionType
AX = mybir.AxisListType.X

P = 128
HEAD = 64
N_Q, N_KV = 8, 2
CONV_K = 3
THETA = 10000.0
EPS = 1e-5
NEG = -1e30
TWO_PI = 2 * np.pi

RAW = 6
SPLIT = 3
UNIT = 2048
CONV_POOL = 2
SCATTER = (6, 7, 3, 1)


def parts_of_two_pi(bits, n):
    rest, found = TWO_PI, []
    for _ in range(n - 1):
        step = 2.0 ** (np.floor(np.log2(rest)) - bits + 1)
        found.append(float(np.floor(rest / step) * step))
        rest -= found[-1]
    return found + [float(np.float32(rest))]


def trunk(nc, x, positions, attn_norm_w, w_in, attn_sinks, conv_w, head_norm_w, w_out, ffn_norm_w,
          dense_w_gate, dense_w_up, dense_w_down, router_w, moe_w_gate, moe_w_up, moe_w_down,
          final_norm_w, out):
    _, S, D = x.shape
    L = w_in.shape[0]
    IN = w_in.shape[2]
    F = dense_w_gate.shape[2]
    E = moe_w_gate.shape[1]
    T = S // P
    K = D // P
    AW = N_Q * HEAD
    CW = D - AW
    V0 = AW + N_KV * HEAD
    B0, C0, H0 = V0 + N_KV * HEAD, V0 + N_KV * HEAD + CW, V0 + N_KV * HEAD + 2 * CW
    NH = D // HEAD
    CH = 512
    STEPS = F // CH
    HALF = HEAD // 2
    assert T == 2 and K == 8 and F % CH == 0 and L == 2 and IN == 4 * CH + CH // 2

    IN_UNITS = 9
    MIX_UNITS = IN_UNITS + 4
    FFN_UNITS = 6 * STEPS
    SMALL = T + 2
    MIX = [0, MIX_UNITS + FFN_UNITS]
    FFN = [MIX_UNITS, 2 * MIX_UNITS + FFN_UNITS]

    with ExitStack() as ctx:
        def sb(name, shape, dt=F32, at=ctx):
            return at.enter_context(nc.sbuf_tensor(name, shape, dt))

        def sem(name):
            return ctx.enter_context(nc.semaphore(name))

        ps = ctx.enter_context(nc.psum_tensor("ps", [P, 8, CH], F32))

        raw = [sb(f"raw{i}", [P, UNIT]) for i in range(RAW)]
        hi = [sb(f"hi{i}", [P, UNIT], F32R) for i in range(SPLIT)]
        lo = [sb(f"lo{i}", [P, UNIT], F32R) for i in range(SPLIT)]
        x_sb = sb("x_sb", [P, T, D])
        xn = sb("xn", [P, T, D])
        xT_hi = sb("xT_hi", [P, K, S], F32R)
        xT_lo = sb("xT_lo", [P, K, S], F32R)
        ident = sb("ident", [P, P])
        mask = sb("mask", [P, 2 * P])
        norm_rows = sb("norm_rows", [3 * L * K, P])
        norm_cols = sb("norm_cols", [P, 3 * L * K])
        w_row = sb("w_row", [P, D])
        sinks = sb("sinks", [P, L, N_Q])
        pos = sb("pos", [P, T], I32)
        freq = sb("freq", [P, HALF])
        ang = sb("ang", [P, T, HALF])
        turns = sb("turns", [P, T, HALF])
        turns_hi = sb("turns_hi", [P, T, HALF])
        cos = sb("cos", [P, T, HALF])
        sin = sb("sin", [P, T, HALF])
        ssq = sb("ssq", [P, T, 2])
        diag = sb("diag", [P, T, P])
        logitsT = sb("logitsT", [E, S])
        var = sb("var", [P, T])
        rstd = sb("rstd", [P, T])
        table = sb("table", [P, T])
        half_neg = sb("half_neg", [P, T])
        ssq_h = sb("ssq_h", [P, T, NH])
        var_h = sb("var_h", [P, T, NH])
        rstd_h = sb("rstd_h", [P, T, NH])
        newton = sb("newton", [P, T, NH])
        smax = sb("smax", [P, T, N_Q])
        m_sb = sb("m_sb", [P, T, N_Q])
        neg_m = sb("neg_m", [P, T, N_Q])
        sink_d = sb("sink_d", [P, T, N_Q])
        sink_e = sb("sink_e", [P, T, N_Q])
        row_sum = sb("row_sum", [P, T, N_Q])
        den = sb("den", [P, T, N_Q])
        rden = sb("rden", [P, T, N_Q])
        router = sb("router", [P, K, E])
        router_hi = sb("router_hi", [P, K, E], F32R)
        router_lo = sb("router_lo", [P, K, E], F32R)
        before = sb("before", [P, P], BF16)
        ones = sb("ones", [P, P], BF16)
        slot_no = sb("slot_no", [P, P])
        expert_no = sb("expert_no", [P, E])
        logits = sb("logits", [P, T, E])
        top = sb("top", [P, T, 8])
        top_at = sb("top_at", [P, T, 8], U32)
        top_f = sb("top_f", [P, T, 2])
        gap = sb("gap", [P, T])
        e2 = sb("e2", [P, T])
        one_e2 = sb("one_e2", [P, T])
        gates = sb("gates", [P, T, 2])
        first = sb("first", [P, T, E])
        second = sb("second", [P, T, E])
        chosen = sb("chosen", [P, T, E])
        chosen_b = sb("chosen_b", [P, T, E], BF16)
        gate = sb("gate", [P, T, 2 * E])
        rank = sb("rank", [P, T, 2 * E + 1])
        rank1 = sb("rank1", [P, T, E])
        count = sb("count", [P, 1])
        passes_i = sb("passes_i", [P, 1], I32)

        mixer_region = ExitStack()
        proj = sb("proj", [P, T, IN], at=mixer_region)
        k_twice = sb("k_twice", [P, T, N_KV, 2, HEAD], at=mixer_region)
        qT = sb("qT", [P, N_Q // 2, S], at=mixer_region)
        kT = sb("kT", [P, N_KV, S], at=mixer_region)
        sc = [sb("sc0", [P, 2, 4, P], at=mixer_region), sb("sc1", [P, 2, 4, 2 * P], at=mixer_region)]
        pT = sb("pT", [P, 3 * N_Q, P], at=mixer_region)
        u_shift = [sb(f"u_shift{i}", [P, T, CW], at=mixer_region) for i in (1, 2)]
        conv_row = sb("conv_row", [P, CONV_K, CW], at=mixer_region)
        squared = sc[1][:].rearrange("p a b c -> p (a b c)").rearrange("p (t d) -> p t d", t=T)
        PT_BANK = (4, 5, 6, 7, 2, 3)
        PT_AT = (8, 12, 16, 20, 0, 4)
        mixer_region.close()
        silu = sb("silu", [P, 1024])
        hid = sb("hid", [P, 1024])
        hT_hi = sb("hT_hi", [P, 4, S], F32R)
        hT_lo = sb("hT_lo", [P, 4, S], F32R)
        t_hi = sb("t_hi", [P, T, D], F32R)
        t_lo = sb("t_lo", [P, T, D], F32R)
        y_hi = sb("y_hi", [P, D], F32R)
        y_lo = sb("y_lo", [P, D], F32R)
        pick = sb("pick", [P, T, P], F32R)
        pickT = sb("pickT", [P, T, P], F32R)

        s_raw = [sem(f"raw_landed{i}") for i in range(RAW)]
        s_hi, s_lo, s_used = sem("hi_written"), sem("lo_written"), sem("unit_used")
        s_x, s_norm_w, s_small = sem("x_landed"), sem("norm_w_landed"), sem("small_landed")
        s_wrow, s_conv = sem("w_row_landed"), sem("conv_w_landed")
        s_const = sem("constants_built")
        s_cols, s_colsb = sem("norm_cols_turned"), sem("norm_cols_copied")
        s_ang, s_trig = sem("angles_ready"), sem("sin_cos_ready")
        s_ssq, s_rstd, s_xn, s_diag = (sem("squares_summed"), sem("rstd_ready"), sem("rows_normed"),
                                       sem("diag_rstd_ready"))
        s_hsq = sem("head_squares_ready")
        s_turn, s_thi, s_tlo = sem("rows_turned"), sem("xT_hi_written"), sem("xT_lo_written")
        s_pjo, s_last, s_rope = sem("proj_copied"), sem("last_chunk_copied"), sem("rope_done")
        s_qkT, s_qkA, s_qkD = sem("qk_turned"), sem("qk_copied_by_act"), sem("qk_copied_by_dve")
        s_score, s_masked, s_negm, s_exp, s_esink = (sem("scores_ready"), sem("scores_masked"), sem("max_ready"),
                                                     sem("exp_done"), sem("sink_exp_done"))
        s_pT, s_pTA, s_pTD = sem("probs_turned"), sem("probsT_copied_by_act"), sem("probsT_copied_by_dve")
        s_o = sem("attention_ready")
        s_u = [sem("conv_input_a"), sem("conv_input_b")]
        s_shift = sem("shift_landed")
        s_conv_done = [sem("conv_done_a"), sem("conv_done_b")]
        s_silu, s_hid = sem("silu_done"), sem("hidden_ready")
        s_hT, s_hhi, s_hlo = sem("hidden_turned"), sem("hT_hi_written"), sem("hT_lo_written")
        s_y0, s_yhi, s_ylo = sem("y_first_half"), sem("y_hi_written"), sem("y_lo_written")
        s_logitT, s_logitTc = sem("logitsT_ready"), sem("logitsT_copied")
        s_rw, s_logit, s_top, s_e2, s_chosen, s_prefix, s_route = (
            sem("router_split"), sem("logits_ready"), sem("top_found"), sem("gap_exp_done"), sem("chosen_ready"),
            sem("prefix_ready"), sem("routes_ready"))
        s_tokn = sem("tokens_normed")
        s_tok, s_tokhi, s_toklo = sem("tokens_scaled"), sem("tokens_hi"), sem("tokens_lo")
        s_pick, s_gath = sem("pick_built"), sem("tokens_gathered")
        s_xhi, s_xlo = sem("xe_hi_written"), sem("xe_lo_written")
        s_pkT, s_pickT, s_scat, s_added = (sem("pick_turned"), sem("pickT_copied"), sem("y_scattered"),
                                           sem("residual_added"))
        s_out = sem("out_stored")
        s_dvec, s_poolc = sem("dve_chain"), sem("pool_chain")

        CHUNK = [(0, CH), (CH, CH), (C0, CH), (H0, CH), (2 * CH, C0 - 2 * CH)]

        CONV_CUT = (0, CONV_POOL * HEAD, CW)

        def turn_bank(j, b):
            return b if j == 3 else 4 + b

        def norm_col(j, k):
            c = K * (L * (j % 3) + j // 3) + k
            return norm_cols[:, c:c + 1]

        def conv_input(eng, l, part):
            a, b = CONV_CUT[part:part + 2]
            u = proj[:, :, C0 + a:C0 + b]
            eng.tensor_tensor(u, u, proj[:, :, H0 + a:H0 + b], ALU.mult).then_inc(s_u[part], 1)

        def conv(eng, link, l, part):
            a, b = CONV_CUT[part:part + 2]
            u = proj[:, :, C0 + a:C0 + b]
            u1, u2 = (us[:, :, a:b] for us in u_shift)

            def tap(i):
                return conv_row[:, i, a:b].unsqueeze(1).to_broadcast([P, T, b - a])

            eng.wait_ge(s_shift, 64 * (l + 1))
            eng.wait_ge(s_conv, 16 * (l + 1))
            eng.tensor_tensor(u2, u2, tap(0), ALU.mult)
            link(eng.tensor_tensor(u1, u1, tap(1), ALU.mult))
            eng.tensor_tensor(u, u, tap(2), ALU.mult)
            link(eng.tensor_tensor(u2, u2, u1, ALU.add))
            link(eng.tensor_tensor(u2, u2, u, ALU.add))
            eng.tensor_tensor(xn[:, :, AW + a:AW + b], proj[:, :, B0 + a:B0 + b], u2,
                              ALU.mult).then_inc(s_conv_done[part], 1)

        def no(u):
            return u[0] + RAW * u[1]

        def load_unit(sp, u, view):
            s, d = u
            if s >= RAW:
                sp.wait_ge(s_lo, no(u) - RAW + 1)
            k = view.shape[1]
            dst = raw[s % RAW][:].rearrange("p (k n) -> p k n", k=k)
            sp.dma_start(dst, view).then_inc(s_raw[s % RAW], 16)

        def split_hi(act, u):
            s, d = u
            act.wait_ge(s_raw[s % RAW], 16 * (s // RAW + 1 + d))
            if s >= SPLIT:
                act.wait_ge(s_used, no(u) - SPLIT + 1)
            act.copy(hi[s % SPLIT][:], raw[s % RAW][:]).then_inc(s_hi, 1)

        def split_lo(dve, u):
            s, d = u
            dve.wait_ge(s_hi, no(u) + 1)
            dve.tensor_tensor(lo[s % SPLIT][:], raw[s % RAW][:], hi[s % SPLIT][:].bitcast(F32),
                              ALU.subtract).then_inc(s_lo, 1)

        def first_step(g):
            return isinstance(g, int) and g == 0

        def halves(u, k):
            s = u[0]
            return [h[s % SPLIT][:].rearrange("p (k n) -> p k n", k=k) for h in (hi, lo)]

        def gate_unit(base, c, h, d=0):
            return (base + h, d) if c == 0 else (base + 4 + h, d)

        def up_unit(base, c, h, d=0):
            return (base + 2 + h, d) if c == 0 else (base + 6 + h, d)

        def down_unit(base, h, d=0):
            return (base + 8 + h, d)

        def last_unit(base, h, d=0):
            return (base + FFN_UNITS - 2 + h, d)

        block = ctx.enter_context(nc.Block())

        @block.sync
        def _(sp):
            def mixer(l):
                src = w_in[l].rearrange("(k p) n -> p k n", p=P)
                for c in range(4):
                    for h in range(1 if l == c == 0 else 0, 2):
                        load_unit(sp, (MIX[l] + 2 * c + h, 0),
                                  src[:, 4 * h:4 * h + 4, CHUNK[c][0]:CHUNK[c][0] + CH])
                load_unit(sp, (MIX[l] + 8, 0), src[:, :, CHUNK[4][0]:sum(CHUNK[4])])
                src = w_out[l].rearrange("(k p) n -> p k n", p=P)
                for c in range(2):
                    for h in range(2):
                        load_unit(sp, (MIX[l] + IN_UNITS + 2 * c + h, 0),
                                  src[:, 4 * h:4 * h + 4, c * CH:(c + 1) * CH])
                for part in range(2):
                    sp.wait_ge(s_u[part], l + 1)
                for i, us in enumerate(u_shift):
                    s = i + 1
                    sp.dma_start(us[s:P, :, :], proj[0:P - s, :, C0:H0]).then_inc(s_shift, 16)
                    sp.dma_start(us[0:s, 1, :], proj[P - s:P, 0, C0:H0]).then_inc(s_shift, 16)

            def swiglu(base, gate_w, up_w, down_w, e, d0):
                def gate_up(c, col, d):
                    for h in range(2):
                        load_unit(sp, gate_unit(base, c, h, d), gate_w[:, bass.ds(K * e + 4 * h, 4), bass.ds(col, CH)])
                    for h in range(2):
                        load_unit(sp, up_unit(base, c, h, d), up_w[:, bass.ds(K * e + 4 * h, 4), bass.ds(col, CH)])

                gate_up(0, 0, d0)
                with sp.Fori(1, STEPS) as c:
                    d = d0 + (c - 1)
                    gate_up(1, CH * c, d)
                    for h in range(2):
                        load_unit(sp, down_unit(base, h, d), down_w[:, bass.ds(e * (F // P) + 4 * c - 4 + 2 * h, 2), :])
                for h in range(2):
                    load_unit(sp, last_unit(base, h, d0),
                              down_w[:, bass.ds(e * (F // P) + F // P - 4 + 2 * h, 2), :])

            load_unit(sp, (0, 0), w_in[0].rearrange("(k p) n -> p k n", p=P)[:, 0:4, 0:CH])
            for i, w in enumerate((attn_norm_w, head_norm_w, ffn_norm_w)):
                sp.dma_start(norm_rows[L * K * i:L * K * (i + 1), :],
                             w.rearrange("l (k p) -> (l k) p", p=P)).then_inc(s_norm_w, 16)
            sp.dma_start(x_sb[:], x.rearrange("a (t p) d -> p (a t) d", p=P)).then_inc(s_x, 16)
            mixer(0)
            swiglu(FFN[0], dense_w_gate.rearrange("l (k p) n -> p (l k) n", p=P),
                   dense_w_up.rearrange("l (k p) n -> p (l k) n", p=P),
                   dense_w_down.rearrange("l (k p) n -> p (l k) n", p=P), 0, 0)
            mixer(1)
            moe = (moe_w_gate.rearrange("l e (k p) n -> p (l e k) n", p=P),
                   moe_w_up.rearrange("l e (k p) n -> p (l e k) n", p=P),
                   moe_w_down.rearrange("l e (k p) n -> p (l e k) n", p=P))
            with sp.Fori(0, E) as e:
                swiglu(FFN[1], *moe, e, STEPS * e)
            sp.wait_ge(s_route, 1)
            passes = sp.value_load(passes_i[0:1, 0:1], min_val=1, max_val=2)
            with sp.If(passes > 1):
                with sp.Fori(0, E) as e:
                    swiglu(FFN[1], *moe, e, STEPS * e + STEPS * E)
            for h in range(2):
                load_unit(sp, (FFN[1] + h, passes * (STEPS * E)), moe[0][:, 4 * h:4 * h + 4, 0:CH])
            for t in range(T):
                sp.wait_ge(s_xn, T * L + t + 1)
                sp.dma_start(out[0, t * P:(t + 1) * P, :], xn[:, t, :]).then_inc(s_out, 16)
            sp.wait_ge(s_out, 16 * T)

        @block.gpsimd
        def _(pool):
            chain = [0]

            def link(ins):
                chain[0] += 1
                ins.then_inc(s_poolc, 1)
                pool.wait_ge(s_poolc, chain[0])

            link(pool.memset(ident[:], 0.0))
            pool.affine_select(ident[:], ident[:], [[-1, P]], ALU.not_equal, 1.0, base=0,
                               channel_multiplier=1).then_inc(s_const, 1)
            inv_freq = np.power(np.float32(THETA), -np.arange(0, HEAD, 2, dtype=np.float32) / np.float32(HEAD))
            for i in range(HALF):
                last = pool.memset(freq[:, i:i + 1], float(inv_freq[i]))
            last.then_inc(s_const, 1)
            pool.memset(half_neg[:], -0.5)
            link(pool.memset(mask[:], 0.0))
            link(pool.affine_select(mask[:], mask[:], [[-1, 2 * P]], ALU.is_ge, NEG, base=P, channel_multiplier=1))
            link(pool.affine_select(mask[:], mask[:], [[1, 2 * P]], ALU.is_gt, NEG, base=0, channel_multiplier=-1))
            link(pool.memset(ones[:], 1.0))
            pool.affine_select(before[:], ones[:], [[1, P]], ALU.is_gt, 0.0, base=0, channel_multiplier=-1)
            pool.iota(slot_no[:], [[1, P]], base=0, channel_multiplier=0, allow_small_or_imprecise_dtypes=True)
            pool.iota(expert_no[:], [[1, E]], base=0, channel_multiplier=0,
                      allow_small_or_imprecise_dtypes=True).then_inc(s_const, 1)

            def rsqrt(i):
                pool.wait_ge(s_ssq, 4 * (i + 1))
                link(pool.tensor_tensor(var[:], ssq[:, :, 0], ssq[:, :, 1], ALU.add))
                link(pool.tensor_scalar(var[:], var[:], 1.0 / D, EPS, ALU.mult, ALU.add))
                pool.tensor_tensor(rstd[:], var[:], half_neg[:], ALU.pow).then_inc(s_rstd, 1)

            for l in range(L):
                rsqrt(2 * l)
                pool.dma_start(conv_row[:], conv_w[l].unsqueeze(0).partition_broadcast(P)).then_inc(s_conv, 16)
                pool.wait_ge(s_pjo, 4 * l + 1)
                for i, us in enumerate(u_shift):
                    pool.memset(us[0:i + 1, 0, :], 0.0)
                pool.wait_ge(s_pjo, 4 * l + 4)
                conv_input(pool, l, 0)
                conv(pool, link, l, 0)
                if l == 0:
                    pool.dma_start(w_row[:], ffn_norm_w[L - 1:L, :].partition_broadcast(P)).then_inc(s_wrow, 16)
                rsqrt(2 * l + 1)
            pool.wait_ge(s_wrow, 16)
            pool.wait_ge(s_tokn, 2)
            pool.wait_ge(s_tok, 1)
            pool.tensor_tensor(xn[:, 1, :], xn[:, 1, :], w_row[:], ALU.mult).then_inc(s_tok, 1)
            pool.wait_ge(s_tokhi, 1)
            pool.tensor_tensor(t_lo[:, 0, :], xn[:, 0, :], t_hi[:, 0, :].bitcast(F32),
                               ALU.subtract).then_inc(s_toklo, 1)
            pool.wait_ge(s_tok, T)
            pool.dma_start(w_row[:], final_norm_w.unsqueeze(0).partition_broadcast(P)).then_inc(s_wrow, 16)
            rsqrt(4)
            pool.wait_ge(s_wrow, 32)

        @block.scalar
        def _(act):
            issued = [0]

            def ahead(n):
                for u in range(issued[0], n):
                    split_hi(act, (u, 0))
                issued[0] = max(issued[0], n)

            def squares(i, n, added=None):
                for t in range(T):
                    if added is None:
                        act.wait_ge(s_x, 16)
                    else:
                        act.wait_ge(s_added, added + T * n + t + 1)
                    cols = slice(n * CH, (n + 1) * CH)
                    act.activation(xn[:, t, cols], x_sb[:, t, cols], ACT.Square,
                                   accum_out=ssq[:, t, n:n + 1]).then_inc(s_ssq, 1)

            def turn_hi(j, banks):
                for b in banks:
                    act.wait_ge(s_turn, 4 * j + b + 1)
                    for i in range(2):
                        k = 2 * b + i
                        last = act.mul(xT_hi[:, k, :], ps[:, turn_bank(j, b), i * S:(i + 1) * S], norm_col(j, k))
                    last.then_inc(s_thi, 1)

            act.wait_ge(s_cols, 1)
            act.copy(norm_cols[:], ps[:, 0, 0:3 * L * K]).then_inc(s_colsb, 1)
            act.wait_ge(s_colsb, 1)
            for t in range(T):
                act.dma_start(pos[:, t:t + 1], positions[0:1, t * P:(t + 1) * P].rearrange("a p -> p a")
                              ).then_inc(s_small, 16)
            act.dma_start(sinks[:].rearrange("p l h -> p (l h)"),
                          attn_sinks.rearrange("(a l) h -> a (l h)", a=1).partition_broadcast(P)).then_inc(s_small, 16)
            act.dma_start(router[:], router_w[0].rearrange("(k p) e -> p k e", p=P)).then_inc(s_small, 16)

            def mixer(l):
                base = MIX[l]
                ahead(base + 1)
                turn_hi(3 * l, range(4))
                ahead(base + 2)
                for n in range(2):
                    squares(2 * l, n, 4 if l else None)
                ahead(base + 3)
                def copy_out(c):
                    act.wait_ge(s_used, base + 2 * c + 2)
                    at = CHUNK[c][0]
                    for t in range(T):
                        last = act.mul(proj[:, t, at:at + CH], ps[:, 2 * (c % 2) + t, :], rstd[:, t:t + 1])
                    last.then_inc(s_pjo, 1)

                def exps(t, heads):
                    for h in heads:
                        s = sc[t][:, h % 2, h // 2, :]
                        last = act.activation(s, s, ACT.Exp, bias=neg_m[:, t, h:h + 1],
                                              accum_out=row_sum[:, t, h:h + 1])
                    last.then_inc(s_exp, 1)

                ahead(base + 4)
                act.wait_ge(s_rstd, 2 * l + 1)
                copy_out(0)
                if l == 0:
                    act.wait_ge(s_ang, 1)
                    act.activation(sin[:], ang[:], ACT.Sin)
                    act.activation(cos[:], turns[:], ACT.Sin).then_inc(s_trig, 1)
                    act.copy(router_hi[:], router[:]).then_inc(s_rw, 1)
                ahead(base + 6)
                copy_out(1)
                ahead(base + 8)
                copy_out(2)
                ahead(base + 9)
                act.wait_ge(s_qkT, l + 1)
                act.mul(qT[:, 0:2, :], ps[:, 4, :], HEAD ** -0.5).then_inc(s_qkA, 1)
                act.copy(kT[:], ps[:, 6, :]).then_inc(s_qkA, 1)
                act.activation(table[:], half_neg[:], ACT.Exp)
                ahead(base + 10)
                act.wait_ge(s_negm, T * l + 1)
                exps(1, range(N_Q // 2))
                copy_out(3)
                exps(1, range(N_Q // 2, N_Q))
                act.wait_ge(s_negm, T * l + 2)
                exps(0, range(N_Q))
                act.activation(sink_e[:], sink_d[:], ACT.Exp).then_inc(s_esink, 1)
                for g in range(0, 6, 2):
                    act.wait_ge(s_pT, 6 * l + g + 1)
                    act.copy(pT[:, PT_AT[g]:PT_AT[g] + 4, :], ps[:, PT_BANK[g], :]).then_inc(s_pTA, 1)
                ahead(base + 12)
                for i, t in enumerate((1, 0)):
                    act.wait_ge(s_o, T * l + i + 1)
                    for h in range(N_Q):
                        cols = slice(h * HEAD, (h + 1) * HEAD)
                        last = act.activation(squared[:, t, cols], ps[:, t, cols], ACT.Square,
                                              accum_out=ssq_h[:, t, h:h + 1])
                    last.then_inc(s_hsq, 1)
                act.wait_ge(s_conv_done[0], l + 1)
                act.wait_ge(s_conv_done[1], l + 1)
                act.activation(squared[:, :, AW:D], xn[:, :, AW:D], ACT.Square).then_inc(s_hsq, 1)
                turn_hi(3 * l + 1, range(4))
                ahead(base + MIX_UNITS + 1)
                squares(2 * l + 1, 0, 8 * l)
                if l == 0:
                    ahead(base + MIX_UNITS + 2)
                    squares(1, 1, 0)
                    turn_hi(2, range(4))
                else:
                    turn_hi(5, range(2))
                    squares(3, 1, 8)
                    turn_hi(5, range(2, 4))

            def silu_step(g, u, dense):
                act.wait_ge(s_used, no(u) + 1)
                if not first_step(g):
                    act.wait_ge(s_hid, g)
                if dense:
                    act.activation(silu[:], ps[:, 0:2, :], ACT.Silu).then_inc(s_silu, 1)
                else:
                    act.activation(silu[:, 0:CH], ps[:, 0, :], ACT.Silu).then_inc(s_silu, 1)

            def hidden_hi(g, prev_down, dense):
                if dense:
                    act.wait_ge(s_hid, g + 1)
                    if prev_down is not None:
                        act.wait_ge(s_used, no(prev_down) + 1)
                    act.copy(hT_hi[:], hid[:]).then_inc(s_hhi, 1)
                else:
                    act.wait_ge(s_hT, g + 1)
                    act.copy(hT_hi[:, :, 0:P], ps[:, 1, :]).then_inc(s_hhi, 1)

            def swiglu(base, g0, d0, dense, pick_e=None):
                ustart = issued[0] - base if dense else 2
                for i in range(ustart, 4):
                    split_hi(act, (base + i, d0))
                silu_step(g0, gate_unit(base, 0, 1, d0), dense)
                if pick_e is not None:
                    act.wait_ge(s_pkT, pick_e + 1)
                    act.copy(pickT[:], ps[:, 7, 0:S]).then_inc(s_pickT, 1)
                split_hi(act, (base + 4, d0))
                split_hi(act, (base + 5, d0))
                with act.Fori(1, STEPS) as c:
                    d = d0 + (c - 1)
                    b = base + 4
                    split_hi(act, (b + 2, d))
                    split_hi(act, (b + 3, d))
                    silu_step(g0 + c, gate_unit(base, 1, 1, d), dense)
                    hidden_hi(d0 + c - 1, (b - 1, d), dense)
                    for i in range(4, 8):
                        split_hi(act, (b + i, d))

            mixer(0)
            swiglu(FFN[0], 0, 0, True)
            hidden_hi(STEPS - 1, (FFN[0] + FFN_UNITS - 3, 0), True)
            issued[0] = FFN[0] + FFN_UNITS
            ahead(FFN[0] + FFN_UNITS + 2)
            mixer(1)

            act.wait_ge(s_rstd, 4)
            for t in range(T):
                act.mul(xn[:, t, :], x_sb[:, t, :], rstd[:, t:t + 1]).then_inc(s_tokn, 1)
            for t in range(T):
                act.wait_ge(s_tok, t + 1)
                act.copy(t_hi[:, t, :], xn[:, t, :]).then_inc(s_tokhi, 1)
            act.wait_ge(s_top, 1)
            act.activation(e2[:], gap[:], ACT.Exp).then_inc(s_e2, 1)

            def gathered_hi(e):
                for i, b in enumerate((7, 6)):
                    act.wait_ge(s_gath, 2 * e + i + 1)
                    act.copy(xT_hi[:, 4 * i:4 * i + 4, 0:P], ps[:, b, :]).then_inc(s_xhi, 1)

            ahead(FFN[1] + 2)
            gathered_hi(0)
            act.wait_ge(s_route, 1)
            passes = act.value_load(passes_i[0:1, 0:1], min_val=1, max_val=2)
            with act.Fori(0, passes * E) as e:
                swiglu(FFN[1], STEPS + STEPS * e, STEPS * e, False, e)
                hidden_hi(STEPS * e + STEPS - 1, None, False)
                gathered_hi(e + 1)
                split_hi(act, (FFN[1] + FFN_UNITS, STEPS * e))
                for h in range(2):
                    if h == 0:
                        act.wait_ge(s_y0, e + 2)
                    else:
                        act.wait_ge(s_used, no(last_unit(FFN[1], 1, STEPS * e)) + 1)
                    act.copy(y_hi[:, h * CH:(h + 1) * CH], ps[:, 4 + h, :]).then_inc(s_yhi, 1)
                split_hi(act, (FFN[1] + FFN_UNITS + 1, STEPS * e))
            for n in range(2):
                squares(4, n, passes * (4 * E) + 8)

        @block.vector
        def _(dve):
            issued = [0]
            chain = [0]

            def ahead(n):
                for u in range(issued[0], n):
                    split_lo(dve, (u, 0))
                issued[0] = max(issued[0], n)

            def link(ins):
                chain[0] += 1
                ins.then_inc(s_dvec, 1)
                dve.wait_ge(s_dvec, chain[0])

            def wide(ap, n):
                return ap.unsqueeze(1).to_broadcast([P, n, ap.shape[1]])

            def rope_tables():
                dve.wait_ge(s_small, 16 * SMALL)
                dve.wait_ge(s_const, 2)
                link(dve.tensor_copy(gap[:], pos[:]))
                for t in range(T):
                    last = dve.tensor_scalar(ang[:, t, :], freq[:], gap[:, t:t + 1], None, ALU.mult)
                link(last)
                magic = 1.5 * 2 ** 23
                link(dve.tensor_scalar(turns[:], ang[:], 1 / TWO_PI, magic, ALU.mult, ALU.add))
                link(dve.tensor_scalar(turns[:], turns[:], magic, None, ALU.subtract))
                link(dve.tensor_scalar(turns_hi[:], turns[:], magic * 4096, None, ALU.add))
                link(dve.tensor_scalar(turns_hi[:], turns_hi[:], magic * 4096, None, ALU.subtract))
                link(dve.tensor_tensor(turns[:], turns[:], turns_hi[:], ALU.subtract))
                for part in parts_of_two_pi(12, 3):
                    for n in (turns_hi, turns):
                        link(dve.scalar_tensor_tensor(ang[:], n[:], -part, ang[:], ALU.mult, ALU.add))
                pi = float(np.nextafter(np.float32(np.pi), np.float32(0)))
                link(dve.tensor_scalar(ang[:], ang[:], pi, -pi, ALU.min, ALU.max))
                link(dve.scalar_tensor_tensor(turns[:], ang[:], -1.0, ang[:], ALU.mult, ALU.max))
                dve.tensor_scalar(turns[:], turns[:], -1.0, float(np.pi / 2), ALU.mult, ALU.add).then_inc(s_ang, 1)

            def turn_lo(j, banks):
                for b in banks:
                    dve.wait_ge(s_thi, 4 * j + b + 1)
                    for i in range(2):
                        k = 2 * b + i
                        last = dve.scalar_tensor_tensor(xT_lo[:, k, :], ps[:, turn_bank(j, b), i * S:(i + 1) * S],
                                                        norm_col(j, k), xT_hi[:, k, :].bitcast(F32),
                                                        ALU.mult, ALU.subtract)
                    last.then_inc(s_tlo, 1)

            def rope(l, t):
                qk = proj[:, t, 0:V0]
                flat = sc[1][:].rearrange("p a b c -> p (a b c)")
                by_cos, by_sin = flat[:, 0:V0], flat[:, V0:2 * V0]
                n = V0 // HALF
                dve.tensor_tensor(by_cos.rearrange("p (n d) -> p n d", d=HALF),
                                  qk.rearrange("p (n d) -> p n d", d=HALF), wide(cos[:, t, :], n), ALU.mult)
                link(dve.tensor_tensor(by_sin.rearrange("p (n d) -> p n d", d=HALF),
                                       qk.rearrange("p (n d) -> p n d", d=HALF), wide(sin[:, t, :], n), ALU.mult))
                c, s, q = (a.rearrange("p (h x d) -> p h x d", x=2, d=HALF) for a in (by_cos, by_sin, qk))
                for x, op in ((0, ALU.subtract), (1, ALU.add)):
                    dve.tensor_tensor(q[:, 0:N_Q, x, :], c[:, 0:N_Q, x, :], s[:, 0:N_Q, 1 - x, :], op)
                    for i in range(2):
                        last = dve.tensor_tensor(k_twice[:, t, :, i, x * HALF:(x + 1) * HALF],
                                                 c[:, N_Q:, x, :], s[:, N_Q:, 1 - x, :], op)
                last.then_inc(s_rope, 1)

            def add(bank, n, stride=1):
                for t in range(T):
                    xs = x_sb[:, t, n * CH:(n + 1) * CH]
                    dve.tensor_tensor(xs, ps[:, bank + stride * t, :], xs, ALU.add).then_inc(s_added, 1)

            def head_rsqrt():
                link(dve.tensor_scalar(var_h[:], ssq_h[:], 1.0 / HEAD, EPS, ALU.mult, ALU.add))
                link(dve.tensor_scalar(rstd_h[:].bitcast(I32), var_h[:].bitcast(I32), -0.5, float(0x5f3759df),
                                       ALU.mult, ALU.add))
                for _ in range(3):
                    link(dve.tensor_tensor(newton[:], rstd_h[:], rstd_h[:], ALU.mult))
                    link(dve.scalar_tensor_tensor(newton[:], newton[:], -0.5, var_h[:], ALU.mult, ALU.mult))
                    link(dve.scalar_tensor_tensor(rstd_h[:], newton[:], 1.5, rstd_h[:], ALU.add, ALU.mult))

            def mixer(l):
                base = MIX[l]
                if l == 0:
                    ahead(1)
                    dve.wait_ge(s_colsb, 1)
                turn_lo(3 * l, range(4))
                ahead(base + 3)
                if l == 0:
                    rope_tables()
                ahead(base + 6)
                dve.wait_ge(s_pjo, 4 * l + 2)
                dve.wait_ge(s_trig, 1)
                for t in range(T):
                    if t:
                        dve.wait_ge(s_rope, T * l + t)
                    rope(l, t)
                    ahead(base + 7 + t)
                if l == 0:
                    dve.wait_ge(s_rw, 1)
                    dve.tensor_tensor(router_lo[:], router[:], router_hi[:].bitcast(F32),
                                      ALU.subtract).then_inc(s_rw, 1)
                dve.wait_ge(s_qkT, l + 1)
                dve.tensor_scalar(qT[:, 2:4, :], ps[:, 5, :], HEAD ** -0.5, None, ALU.mult).then_inc(s_qkD, 1)
                ahead(base + 9)
                dve.wait_ge(s_score, 3 * l + 1)
                dve.tensor_tensor(sc[0][:, 0], ps[:, 0, :], wide(mask[:, P:2 * P], 4), ALU.add)
                dve.tensor_tensor(sc[0][:, 1], ps[:, 1, :], wide(mask[:, P:2 * P], 4), ALU.add).then_inc(s_masked, 1)
                for i in range(2):
                    dve.wait_ge(s_score, 3 * l + 2 + i)
                    dve.tensor_tensor(sc[1][:, 0, 2 * i:2 * i + 2], ps[:, 4 + i, :], wide(mask[:], 2), ALU.add)
                    last = dve.tensor_tensor(sc[1][:, 1, 2 * i:2 * i + 2], ps[:, 6 + i, :], wide(mask[:], 2),
                                             ALU.add)
                link(last)
                for t in (1, 0):
                    if t == 0:
                        dve.wait_ge(s_masked, l + 1)
                    link(dve.tensor_reduce(smax[:, t, :].rearrange("p (i x) -> p x i", x=2), sc[t][:], AX, ALU.max))
                    link(dve.tensor_tensor(m_sb[:, t, :], smax[:, t, :], sinks[:, l, :], ALU.max))
                    link(dve.tensor_scalar(neg_m[:, t, :], m_sb[:, t, :], -1.0, None, ALU.mult))
                    dve.tensor_tensor(sink_d[:, t, :], sinks[:, l, :], neg_m[:, t, :], ALU.add).then_inc(s_negm, 1)
                ahead(base + 10)
                dve.wait_ge(s_pjo, 4 * l + 4)
                conv_input(dve, l, 1)
                dve.wait_ge(s_used, base + IN_UNITS)
                at, width = CHUNK[4]
                for t in range(T):
                    last = dve.tensor_scalar(proj[:, t, at:at + width], ps[:, t, 0:width], rstd[:, t:t + 1], None,
                                             ALU.mult)
                last.then_inc(s_last, 1)
                dve.wait_ge(s_last, l + 1)
                for g in range(1, 6, 2):
                    dve.wait_ge(s_pT, 6 * l + g + 1)
                    dve.tensor_copy(pT[:, PT_AT[g]:PT_AT[g] + 4, :], ps[:, PT_BANK[g], :]).then_inc(s_pTD, 1)
                dve.wait_ge(s_exp, 3 * (l + 1))
                dve.wait_ge(s_esink, l + 1)
                link(dve.tensor_tensor(den[:], row_sum[:], sink_e[:], ALU.add))
                link(dve.reciprocal(rden[:], den[:]))
                link(dve.tensor_tensor(den[:], rden[:], rden[:], ALU.mult))
                conv(dve, link, l, 1)
                dve.wait_ge(s_hsq, 3 * l + 2)
                dve.tensor_tensor(ssq_h[:, :, 0:N_Q], ssq_h[:, :, 0:N_Q], den[:], ALU.mult)
                dve.wait_ge(s_hsq, 3 * l + 3)
                link(dve.tensor_reduce(ssq_h[:, :, N_Q:NH], squared[:, :, AW:D].rearrange(
                    "p t (h d) -> p t h d", d=HEAD), AX, ALU.add))
                head_rsqrt()
                link(dve.tensor_tensor(rden[:], rden[:], rstd_h[:, :, 0:N_Q], ALU.mult))
                for src, dst, scale in ((ps[:, 0:T, :], xn[:, :, 0:AW], rden[:]),
                                        (xn[:, :, AW:D], xn[:, :, AW:D], rstd_h[:, :, N_Q:NH])):
                    src, dst = (a.rearrange("p t (h d) -> p t h d", d=HEAD) for a in (src, dst))
                    dve.tensor_tensor(dst, src, scale.unsqueeze(3).to_broadcast([P, T, N_Q, HEAD]),
                                      ALU.mult).then_inc(s_xn, 1)
                turn_lo(3 * l + 1, range(4))
                for n in range(2):
                    ahead(base + (MIX_UNITS if n == 0 else MIX_UNITS + 2 - l))
                    if l == 1 and n == 1:
                        turn_lo(5, range(2))
                    dve.wait_ge(s_used, base + IN_UNITS + 2 * n + 2)
                    add(2 * n, n)
                if l == 0:
                    dve.wait_ge(s_rstd, 2)
                    for t in range(T):
                        last = dve.tensor_scalar(diag[:, t, :], ident[:], rstd[:, t:t + 1], None, ALU.mult)
                    last.then_inc(s_diag, 1)
                    turn_lo(2, range(4))
                else:
                    turn_lo(5, range(2, 4))

            def hidden(g, u, dense):
                dve.wait_ge(s_used, no(u) + 1)
                dve.wait_ge(s_silu, g + 1)
                if not first_step(g):
                    dve.wait_ge(s_hlo, g)
                if dense:
                    dve.tensor_tensor(hid[:], ps[:, 2:4, :], silu[:], ALU.mult).then_inc(s_hid, 1)
                else:
                    dve.tensor_tensor(hid[:, 0:CH], ps[:, 2, :], silu[:, 0:CH], ALU.mult).then_inc(s_hid, 1)

            def hidden_lo(g, dense):
                dve.wait_ge(s_hhi, g + 1)
                if dense:
                    dve.tensor_tensor(hT_lo[:], hid[:], hT_hi[:].bitcast(F32), ALU.subtract).then_inc(s_hlo, 1)
                else:
                    dve.tensor_tensor(hT_lo[:, :, 0:P], ps[:, 1, :], hT_hi[:, :, 0:P].bitcast(F32),
                                      ALU.subtract).then_inc(s_hlo, 1)

            def swiglu(base, g0, d0, dense, between=None):
                ustart = issued[0] - base if dense else 2
                for i in range(ustart, 4):
                    split_lo(dve, (base + i, d0))
                split_lo(dve, (base + 4, d0))
                if between:
                    between()
                split_lo(dve, (base + 5, d0))
                hidden(g0, up_unit(base, 0, 1, d0), dense)
                with dve.Fori(1, STEPS) as c:
                    d = d0 + (c - 1)
                    b = base + 4
                    split_lo(dve, (b + 2, d))
                    split_lo(dve, (b + 3, d))
                    hidden_lo(g0 + c - 1, dense)
                    split_lo(dve, (b + 4, d))
                    split_lo(dve, (b + 5, d))
                    hidden(g0 + c, up_unit(base, 1, 1, d), dense)
                    split_lo(dve, (b + 6, d))
                    split_lo(dve, (b + 7, d))

            mixer(0)
            swiglu(FFN[0], 0, 0, True)
            hidden_lo(STEPS - 1, True)
            issued[0] = FFN[0] + FFN_UNITS
            ahead(FFN[0] + FFN_UNITS + 2)
            dve.wait_ge(s_y0, 1)
            add(4, 0, 2)
            dve.wait_ge(s_used, FFN[0] + FFN_UNITS)
            add(5, 1, 2)
            mixer(1)

            dve.wait_ge(s_wrow, 16)
            dve.wait_ge(s_tokn, 1)
            dve.tensor_tensor(xn[:, 0, :], xn[:, 0, :], w_row[:], ALU.mult).then_inc(s_tok, 1)
            dve.wait_ge(s_logitT, 1)
            dve.tensor_copy(logitsT[:], ps[0:E, 0, 0:S]).then_inc(s_logitTc, 1)
            dve.wait_ge(s_logit, 1)
            dve.wait_ge(s_rstd, 4)
            for t in range(T):
                last = dve.tensor_scalar(logits[:, t, :], ps[:, 2, t * E:(t + 1) * E], rstd[:, t:t + 1], None,
                                         ALU.mult)
            link(last)
            for t in range(T):
                last = dve.max(top[:, t, :], logits[:, t, :])
            link(last)
            for t in range(T):
                last = dve.max_index(top_at[:, t, :], top[:, t, :], logits[:, t, :])
            dve.tensor_tensor(gap[:], top[:, :, 1], top[:, :, 0], ALU.subtract).then_inc(s_top, 1)
            link(last)
            link(dve.tensor_copy(top_f[:], top_at[:, :, 0:2]))
            for t in range(T):
                dve.tensor_scalar(first[:, t, :], expert_no[:], top_f[:, t, 0:1], None, ALU.is_equal)
                last = dve.tensor_scalar(second[:, t, :], expert_no[:], top_f[:, t, 1:2], None, ALU.is_equal)
            link(last)
            link(dve.tensor_tensor(chosen[:], first[:], second[:], ALU.add))
            dve.tensor_copy(chosen_b[:], chosen[:]).then_inc(s_chosen, 1)
            dve.memset(rank[:], -1.0)
            dve.wait_ge(s_prefix, 1)
            link(dve.tensor_scalar(rank1[:], ps[:, 1, 0:T * E].rearrange("p (t e) -> p t e", t=T), 1.0, None, ALU.add))
            link(dve.tensor_tensor(rank1[:], rank1[:], chosen[:], ALU.mult))
            dve.tensor_scalar(rank[:, :, E:2 * E], rank1[:], -1.0 - P, None, ALU.add)
            link(dve.tensor_scalar(rank[:, :, 0:E], rank1[:], -1.0, None, ALU.add))

            def build_pick(e):
                for t in range(T):
                    last = dve.tensor_scalar(pick[:, t, :], slot_no[:], rank[:, t, bass.ds(e, 1)], None, ALU.is_equal)
                last.then_inc(s_pick, 1)

            def gathered_lo(e):
                for i, b in enumerate((7, 6)):
                    dve.wait_ge(s_xhi, 2 * e + i + 1)
                    dve.tensor_tensor(xT_lo[:, 4 * i:4 * i + 4, 0:P], ps[:, b, :],
                                      xT_hi[:, 4 * i:4 * i + 4, 0:P].bitcast(F32), ALU.subtract).then_inc(s_xlo, 1)

            build_pick(0)
            dve.wait_ge(s_tokhi, 2)
            dve.tensor_tensor(t_lo[:, 1, :], xn[:, 1, :], t_hi[:, 1, :].bitcast(F32),
                              ALU.subtract).then_inc(s_toklo, 1)
            ahead(FFN[1] + 2)
            link(dve.tensor_reduce(count[:], ps[:, 1, T * E:(T + 1) * E], AX, ALU.max))
            link(dve.tensor_scalar(passes_i[:], count[:], float(P), 1.0, ALU.is_gt, ALU.add))
            dve.memset(count[:], 0.0).then_inc(s_route, 1)
            dve.wait_ge(s_e2, 1)
            link(dve.tensor_scalar(one_e2[:], e2[:], 1.0, None, ALU.add))
            link(dve.reciprocal(gates[:, :, 0], one_e2[:]))
            link(dve.tensor_tensor(gates[:, :, 1], gates[:, :, 0], e2[:], ALU.mult))
            for t in range(T):
                last = dve.tensor_scalar(gate[:, t, 0:E], first[:, t, :], gates[:, t, 0:1], None, ALU.mult)
            link(last)
            for t in range(T):
                last = dve.scalar_tensor_tensor(gate[:, t, 0:E], second[:, t, :], gates[:, t, 1:2],
                                                gate[:, t, 0:E], ALU.mult, ALU.add)
            link(last)
            link(dve.tensor_copy(gate[:, :, E:2 * E], gate[:, :, 0:E]))
            gathered_lo(0)
            passes = dve.value_load(passes_i[0:1, 0:1], min_val=1, max_val=2)
            with dve.Fori(0, passes * E) as e:
                def next_pick():
                    dve.wait_ge(s_pkT, e + 1)
                    build_pick(e + 1)

                swiglu(FFN[1], STEPS + STEPS * e, STEPS * e, False, next_pick)
                hidden_lo(STEPS + STEPS * e + STEPS - 1, False)
                gathered_lo(e + 1)
                split_lo(dve, (FFN[1] + FFN_UNITS, STEPS * e))
                for h in range(2):
                    dve.wait_ge(s_yhi, 2 * e + h + 1)
                    dve.tensor_tensor(y_lo[:, h * CH:(h + 1) * CH], ps[:, 4 + h, :],
                                      y_hi[:, h * CH:(h + 1) * CH].bitcast(F32), ALU.subtract).then_inc(s_ylo, 1)
                dve.wait_ge(s_added, 4 * e + 12)
                for h in range(2):
                    for t in range(T):
                        i = T * h + t
                        dve.wait_ge(s_scat, 4 * e + i + 1)
                        xs = x_sb[:, t, h * CH:(h + 1) * CH]
                        dve.scalar_tensor_tensor(xs, ps[:, SCATTER[i], :], gate[:, t, bass.ds(e, 1)], xs,
                                                 ALU.mult, ALU.add).then_inc(s_added, 1)
                split_lo(dve, (FFN[1] + FFN_UNITS + 1, STEPS * e))
            dve.wait_ge(s_rstd, 5)
            dve.wait_ge(s_wrow, 32)
            for t in range(T):
                dve.scalar_tensor_tensor(xn[:, t, :], x_sb[:, t, :], rstd[:, t:t + 1], w_row[:],
                                         ALU.mult, ALU.mult).then_inc(s_xn, 1)

        @block.tensor
        def _(pe):
            def three(out_ap, a_hi, a_lo, b_hi, b_lo, start, stop, **kw):
                pe.matmul(out_ap, a_hi, b_hi, start=start, stop=False, **kw)
                pe.matmul(out_ap, a_hi, b_lo, start=False, stop=False, **kw)
                return pe.matmul(out_ap, a_lo, b_hi, start=False, stop=stop, **kw)

            def ready(u):
                pe.wait_ge(s_lo, no(u) + 1)

            def turn(j, half):
                kind = j % 3
                if j:
                    pe.wait_ge(s_tlo, 4 * j)
                if kind == 1:
                    pe.wait_ge(s_xn, T * (j // 3) + half + 1)
                elif j == 2:
                    pe.wait_ge(s_diag, 1)
                elif j:
                    pe.wait_ge(s_added, (4 if j == 3 else 8) + T * (half + 1))
                for k in range(4 * half, 4 * half + 4):
                    for t in range(T):
                        o = ps[:, turn_bank(j, k // 2), (k % 2) * S + t * P:(k % 2) * S + (t + 1) * P]
                        cols = slice(k * P, (k + 1) * P)
                        if j == 2:
                            mm = pe.matmul(o, x_sb[:, t, cols], diag[:, t, :], start=True, stop=True)
                        else:
                            mm = pe.transpose(o, (xn if kind == 1 else x_sb)[:, t, cols], ident[:])
                    if k % 2:
                        mm.then_inc(s_turn, 1)

            def rows_product(j, u, k0, nk, banks, first, last):
                ready(u)
                pe.wait_ge(s_tlo, 4 * j + (k0 + nk) // 2)
                uh, ul = halves(u, nk)
                for t in range(T):
                    for k in range(nk):
                        a = slice(t * P, (t + 1) * P)
                        mm = three(ps[:, banks[t], 0:uh.shape[2]], xT_hi[:, k0 + k, a], xT_lo[:, k0 + k, a],
                                   uh[:, k], ul[:, k], first and k == 0, last and k == nk - 1)
                mm.then_inc(s_used, 1)

            def mixer(l):
                base = MIX[l]
                if l == 0:
                    pe.wait_ge(s_x, 16)
                for half in range(2):
                    turn(3 * l, half)
                def chunk(c, h):
                    banks = [2 * (c % 2) + t for t in range(T)]
                    if h == 0 and c in (2, 3):
                        pe.wait_ge(s_pjo, 4 * l + c - 1)
                    if c < 4:
                        rows_product(3 * l, (base + 2 * c + h, 0), 4 * h, 4, banks, h == 0, h == 1)
                    else:
                        pe.wait_ge(s_masked, l + 1)
                        rows_product(3 * l, (base + 8, 0), 0, 8, banks, True, True)

                for c in range(3):
                    for h in range(2):
                        chunk(c, h)
                for t in range(T):
                    pe.wait_ge(s_rope, T * l + t + 1)
                    for i in range(4):
                        pe.transpose(ps[:, 4 + i // 2, (i % 2) * S + t * P:(i % 2) * S + (t + 1) * P],
                                     proj[:, t, i * P:(i + 1) * P], ident[:])
                    for i in range(N_KV):
                        mm = pe.transpose(ps[:, 6, i * S + t * P:i * S + (t + 1) * P],
                                          k_twice[:, t, i].rearrange("p a d -> p (a d)"), ident[:])
                mm.then_inc(s_qkT, 1)
                chunk(3, 0)
                pe.wait_ge(s_qkA, 2 * (l + 1))
                pe.wait_ge(s_qkD, l + 1)
                pe.wait_ge(s_pjo, 4 * l + 3)
                for t in range(T):
                    for i in range(4):
                        for x in range(2):
                            rows = slice(x * HEAD, (x + 1) * HEAD)
                            if t == 0:
                                o = ps[:, x, i * P:(i + 1) * P]
                            else:
                                o = ps[:, 4 + 2 * x + i // 2, (i % 2) * S:(i % 2 + 1) * S]
                            mm = pe.matmul(o, qT[rows, i, t * P:(t + 1) * P], kT[rows, i // 2, 0:(t + 1) * P],
                                           start=True, stop=True)
                        if (t == 0 and i == 3) or (t == 1 and i % 2):
                            mm.then_inc(s_score, 1)
                chunk(3, 1)
                chunk(4, 0)
                pe.wait_ge(s_pjo, 4 * l + 4)
                for g in range(6):
                    t = 1 if g < 4 else 0
                    if g % 4 == 0:
                        pe.wait_ge(s_exp, 3 * l + 3 - t)
                    for m in range(4):
                        n = PT_AT[g] - N_Q * t + m
                        h, kt = n // (t + 1), n % (t + 1)
                        mm = pe.transpose(ps[:, PT_BANK[g], m * P:(m + 1) * P],
                                          sc[t][:, h % 2, h // 2, kt * P:(kt + 1) * P], ident[:])
                    mm.then_inc(s_pT, 1)
                pe.wait_ge(s_last, l + 1)
                for i, t in enumerate((1, 0)):
                    pe.wait_ge(s_pTA, 3 * l + 2 + i)
                    pe.wait_ge(s_pTD, 3 * l + 2 + i)
                    for h in range(N_Q):
                        for kt in range(t + 1):
                            v = proj[:, kt, V0 + h // 4 * HEAD:V0 + (h // 4 + 1) * HEAD]
                            mm = pe.matmul(ps[:, t, h * HEAD:(h + 1) * HEAD],
                                           pT[:, N_Q * t + h * (t + 1) + kt, :], v, start=kt == 0, stop=kt == t)
                    mm.then_inc(s_o, 1)
                for half in range(2):
                    turn(3 * l + 1, half)
                for n in range(2):
                    rows_product(3 * l + 1, (base + IN_UNITS + 2 * n, 0), 0, 4, [2 * n, 2 * n + 1], True, False)
                    if l and n:
                        turn(5, 0)
                    rows_product(3 * l + 1, (base + IN_UNITS + 2 * n + 1, 0), 4, 4, [2 * n, 2 * n + 1], False, True)
                if l == 0:
                    turn(2, 0)
                    turn(2, 1)
                else:
                    turn(5, 1)

            def dense_half(u, h, b0):
                ready(u)
                uh, ul = halves(u, 4)
                for j in range(4):
                    for k in range(4):
                        xk = 4 * h + k
                        w = slice(j * P, (j + 1) * P)
                        o = ps[:, b0 + j // 2, (j % 2) * S:(j % 2 + 1) * S]
                        mm = three(o, uh[:, k, w], ul[:, k, w], xT_hi[:, xk, :], xT_lo[:, xk, :],
                                   h == 0 and k == 0 and j % 2 == 0, h == 1 and k == 3, skip_group_check=True)
                mm.then_inc(s_used, 1)

            def dense_down(u, h, start, stop):
                ready(u)
                uh, ul = halves(u, 2)
                for n in range(2):
                    for t in range(T):
                        for i in range(2):
                            a = hT_hi[:, 2 * h + i, t * P:(t + 1) * P], hT_lo[:, 2 * h + i, t * P:(t + 1) * P]
                            w = slice(n * CH, (n + 1) * CH)
                            mm = three(ps[:, 4 + 2 * t + n, :], *a, uh[:, i, w], ul[:, i, w],
                                       start and h == 0 and i == 0, stop and h == 1 and i == 1)
                    if stop and h == 1 and n == 0:
                        mm.then_inc(s_y0, 1)
                mm.then_inc(s_used, 1)

            def expert_half(u, h, b):
                ready(u)
                uh, ul = halves(u, 4)
                for k in range(4):
                    xk = 4 * h + k
                    mm = three(ps[:, b, :], xT_hi[:, xk, 0:P], xT_lo[:, xk, 0:P], uh[:, k], ul[:, k],
                               h == 0 and k == 0, h == 1 and k == 3)
                mm.then_inc(s_used, 1)

            def expert_down(u, h, start, stop):
                ready(u)
                uh, ul = halves(u, 2)
                for n in range(2):
                    for i in range(2):
                        w = slice(n * CH, (n + 1) * CH)
                        mm = three(ps[:, 4 + n, :], hT_hi[:, 2 * h + i, 0:P], hT_lo[:, 2 * h + i, 0:P],
                                   uh[:, i, w], ul[:, i, w], start and h == 0 and i == 0, stop and h == 1 and i == 1)
                    if stop and h == 1 and n == 0:
                        mm.then_inc(s_y0, 1)
                mm.then_inc(s_used, 1)

            def turn_hidden(g):
                pe.wait_ge(s_hid, g + 1)
                for j in range(4):
                    mm = pe.transpose(ps[:, 1, j * P:(j + 1) * P], hid[:, j * P:(j + 1) * P], ident[:])
                mm.then_inc(s_hT, 1)

            def step(base, c, g, d, dense, start_down=None, pick_e=None):
                half = dense_half if dense else expert_half
                if not first_step(g):
                    pe.wait_ge(s_silu, g)
                half(gate_unit(base, c, 0, d), 0, 0)
                if dense and c == 0:
                    pe.wait_ge(s_tlo, 12)
                half(gate_unit(base, c, 1, d), 1, 0)
                if pick_e is not None:
                    pe.wait_ge(s_added, 4 * pick_e + 12)
                    for t in range(T):
                        mm = pe.transpose(ps[:, 7, t * P:(t + 1) * P], pick[:, t, :].bitcast(F32), ident[:])
                    mm.then_inc(s_pkT, 1)
                if c and not dense:
                    turn_hidden(g - 1)
                if not first_step(g):
                    pe.wait_ge(s_hid, g)
                half(up_unit(base, c, 0, d), 0, 2)
                half(up_unit(base, c, 1, d), 1, 2)
                if c:
                    down = dense_down if dense else expert_down
                    pe.wait_ge(s_hlo, g)
                    for h in range(2):
                        down(down_unit(base, h, d), h, start_down, False)

            def swiglu(base, g0, d0, dense, pick_e=None):
                step(base, 0, g0, d0, dense, pick_e=pick_e)
                step(base, 1, g0 + 1, d0, dense, True)
                with pe.Fori(2, STEPS) as c:
                    step(base, 2, g0 + c, d0 + (c - 1), dense, False)

            pe.wait_ge(s_const, 1)
            pe.wait_ge(s_norm_w, 16 * 3)
            pe.transpose(ps[:, 0, 0:3 * L * K], norm_rows[:], ident[0:3 * L * K, 0:3 * L * K]).then_inc(s_cols, 1)
            pe.wait_ge(s_colsb, 1)
            mixer(0)
            pe.wait_ge(s_tlo, 10)
            swiglu(FFN[0], 0, 0, True)
            pe.wait_ge(s_hlo, STEPS)
            dense_down(last_unit(FFN[0], 0), 0, False, True)
            dense_down(last_unit(FFN[0], 1), 1, False, True)
            mixer(1)

            pe.wait_ge(s_rw, 2)
            for k in range(K):
                pe.wait_ge(s_tlo, 20 + k // 2 + 1)
                mm = three(ps[0:E, 0, 0:S], router_hi[:, k, :], router_lo[:, k, :], xT_hi[:, k, :], xT_lo[:, k, :],
                           k == 0, k == K - 1)
            mm.then_inc(s_logitT, 1)
            pe.wait_ge(s_logitTc, 1)
            for t in range(T):
                mm = pe.transpose(ps[:, 2, t * E:(t + 1) * E], logitsT[:, t * P:(t + 1) * P], ident[0:E, 0:E])
            mm.then_inc(s_logit, 1)
            pe.wait_ge(s_chosen, 1)
            pe.wait_ge(s_const, 3)
            pe.matmul(ps[:, 1, 0:E], before[:], chosen_b[:, 0, :], start=True, stop=True)
            pe.matmul(ps[:, 1, E:2 * E], ones[:], chosen_b[:, 0, :], start=True, stop=False)
            pe.matmul(ps[:, 1, E:2 * E], before[:], chosen_b[:, 1, :], start=False, stop=True)
            pe.matmul(ps[:, 1, 2 * E:3 * E], ones[:], chosen_b[:, 0, :], start=True, stop=False)
            pe.matmul(ps[:, 1, 2 * E:3 * E], ones[:], chosen_b[:, 1, :], start=False, stop=True).then_inc(s_prefix, 1)

            def gather(e):
                pe.wait_ge(s_pick, e + 1)
                for i, b in enumerate((7, 6)):
                    for k in range(4):
                        cols = slice((4 * i + k) * P, (4 * i + k + 1) * P)
                        for t in range(T):
                            pe.matmul(ps[:, b, k * P:(k + 1) * P], t_hi[:, t, cols], pick[:, t, :],
                                      start=t == 0, stop=False)
                            mm = pe.matmul(ps[:, b, k * P:(k + 1) * P], t_lo[:, t, cols], pick[:, t, :],
                                           start=False, stop=t == T - 1)
                    mm.then_inc(s_gath, 1)

            pe.wait_ge(s_toklo, T)
            gather(0)
            pe.wait_ge(s_route, 1)
            passes = pe.value_load(passes_i[0:1, 0:1], min_val=1, max_val=2)
            with pe.Fori(0, passes * E) as e:
                pe.wait_ge(s_xlo, 2 * e + 2)
                swiglu(FFN[1], STEPS + STEPS * e, STEPS * e, False, e)
                turn_hidden(STEPS + STEPS * e + STEPS - 1)
                pe.wait_ge(s_pickT, e + 1)
                gather(e + 1)
                pe.wait_ge(s_hlo, STEPS + STEPS * e + STEPS)
                expert_down(last_unit(FFN[1], 0, STEPS * e), 0, False, True)
                expert_down(last_unit(FFN[1], 1, STEPS * e), 1, False, True)
                for h in range(2):
                    pe.wait_ge(s_ylo, 2 * e + h + 1)
                    for t in range(T):
                        i = T * h + t
                        if i == 0:
                            pe.wait_ge(s_xlo, 2 * e + 4)
                        cols = slice(h * CH, (h + 1) * CH)
                        pe.matmul(ps[:, SCATTER[i], :], pickT[:, t, :], y_hi[:, cols], start=True, stop=False)
                        pe.matmul(ps[:, SCATTER[i], :], pickT[:, t, :], y_lo[:, cols], start=False,
                                  stop=True).then_inc(s_scat, 1)


_INS = ["x", "positions", "attn_norm_w", "w_in", "attn_sinks", "conv_w", "head_norm_w", "w_out", "ffn_norm_w",
        "dense_w_gate", "dense_w_up", "dense_w_down", "router_w", "moe_w_gate", "moe_w_up", "moe_w_down",
        "final_norm_w"]


def kernel(**inputs):
    import concourse.bacc as _bacc
    from concourse.bass_utils import run_bass_kernel_spmd as _run

    nc = _bacc.Bacc("TRN2", target_bir_lowering=False, num_devices=1)
    arrays, args = {}, []
    for name in _INS:
        a = np.ascontiguousarray(inputs[name])
        arrays[f"in_{name}"] = a
        args.append(nc.dram_tensor(f"in_{name}", a.shape, mybir.dt.from_np(a.dtype), kind="ExternalInput").ap())
    out = nc.dram_tensor("out_0", inputs["x"].shape, F32, kind="ExternalOutput").ap()
    trunk(nc, *args, out)
    r = _run(nc, [arrays], core_ids=[0])
    return r.results[0]["out_0"]
```
